# Optimizing a Trainium2 kernel written in Bass

```python
import math
import jax, jax.numpy as jnp
from jax import lax
import numpy as np

D_MODEL = 1024
BATCH = 1
SEQ = 1024
DEPTH = 2
DEC_BATCH = 8
DEC_SEQ = 4
PAST_LEN = 2048
PAGE_SIZE = 128

HEAD_DIM = 64
SSD_HEADS = 8
SSD_INNER = SSD_HEADS * HEAD_DIM
SSD_GROUPS = 2
SSD_STATE = 64
SSD_CONV_W = 4
SSD_CONV_DIM = SSD_INNER + 2 * SSD_GROUPS * SSD_STATE
SSD_CHUNK = 128
ATT_HEADS = 4
ATT_WIDTH = ATT_HEADS * HEAD_DIM
IDX_HEADS = 4
IDX_DIM = 64
TOPK_MAX = 256
Q_BLOCK = 128
ROPE_THETA = 10000.0
CC_GROUPS = 4
CC_WIDTH = CC_GROUPS * HEAD_DIM
CC_CONV_W = 31
MIX_WIDTH = SSD_INNER + ATT_WIDTH + CC_WIDTH
D_FF = 2816
FFN_CONV_W = 3
ALPHA = (2 * DEPTH) ** 0.25
BETA = (8 * DEPTH) ** -0.25
EPS = 1e-5
IN_SIZES = (SSD_INNER, SSD_CONV_DIM, SSD_HEADS,
            ATT_WIDTH, ATT_WIDTH, ATT_WIDTH,
            IDX_HEADS * IDX_DIM, IDX_DIM, IDX_HEADS,
            2 * CC_WIDTH)
D_IN = sum(IN_SIZES)

kernel_name = 'hybrid_ssd_dsa_conformer_decoder_step'

def layer_norm(x, g, b):
    xf = x.astype(jnp.float32)
    mu = jnp.mean(xf, -1, keepdims=True)
    var = jnp.mean(jnp.square(xf - mu), -1, keepdims=True)
    return ((xf - mu) * lax.rsqrt(var + EPS) * g.astype(jnp.float32) + b.astype(jnp.float32)).astype(x.dtype)

def rms_norm(x, g):
    xf = x.astype(jnp.float32)
    return (xf * lax.rsqrt(jnp.mean(xf * xf, -1, keepdims=True) + EPS) * g.astype(jnp.float32)).astype(x.dtype)

def rope(x, pos):
    half = x.shape[-1] // 2
    inv = ROPE_THETA ** (-jnp.arange(half, dtype=jnp.float32) / half)
    ang = pos.astype(jnp.float32)[:, None] * inv[None, :]
    cos = jnp.cos(ang)[:, None, :].astype(x.dtype)
    sin = jnp.sin(ang)[:, None, :].astype(x.dtype)
    x1, x2 = x[..., :half], x[..., half:]
    return jnp.concatenate([x1 * cos - x2 * sin, x2 * cos + x1 * sin], axis=-1)

def causal_dwconv(x, prev, w, b):
    xp = jnp.concatenate([prev.astype(x.dtype), x], axis=1)
    y = lax.conv_general_dilated(xp, w[:, None, :].astype(x.dtype), window_strides=(1,), padding='VALID',
                                 dimension_numbers=('NWC', 'WIO', 'NWC'), feature_group_count=x.shape[-1])
    return y + b, xp[:, x.shape[1]:]

def ssd_scan(x, dt, a, bm, cm, h0):
    bsz, length, n_h, _ = x.shape
    q = SSD_CHUNK if length % SSD_CHUNK == 0 else length
    nc = length // q
    rep = n_h // bm.shape[2]
    bh = jnp.repeat(bm, rep, axis=2)
    ch = jnp.repeat(cm, rep, axis=2)
    xdt = x * dt[..., None]
    da = dt * a
    causal = jnp.tril(jnp.ones((q, q), bool))[None, :, :, None]

    def chunks(t):
        return t.reshape(bsz, nc, q, *t.shape[2:]).swapaxes(0, 1)

    def step(h, inp):
        xc, dac, bc, cc = inp
        cum = jnp.cumsum(dac, axis=1)
        seg = cum[:, :, None, :] - cum[:, None, :, :]
        decay = jnp.exp(jnp.where(causal, seg, -jnp.inf))
        cb = jnp.einsum('bthn,bshn->btsh', cc, bc) * decay
        y = jnp.einsum('btsh,bshp->bthp', cb, xc)
        y = y + jnp.einsum('bthn,bhpn->bthp', cc, h) * jnp.exp(cum)[..., None]
        last = cum[:, -1]
        w_s = jnp.exp(last[:, None, :] - cum)
        h = h * jnp.exp(last)[:, :, None, None] + jnp.einsum('bshn,bshp->bhpn', bc * w_s[..., None], xc)
        return h, y

    h, ys = lax.scan(step, h0, (chunks(xdt), chunks(da), chunks(bh), chunks(ch)))
    return ys.swapaxes(0, 1).reshape(x.shape), h

def index_select(qi, wi, ki, q_pos, k_top):
    n_keys = ki.shape[1]
    s = jnp.einsum('bthd,bsd->bths', qi, ki).astype(jnp.float32) * IDX_DIM ** -0.5
    score = jnp.einsum('bths,bth->bts', jax.nn.relu(s), wi.astype(jnp.float32) * IDX_HEADS ** -0.5)
    admissible = jnp.arange(n_keys)[None, None, :] <= q_pos[None, :, None]
    score = jnp.where(admissible, score, -jnp.inf)
    vals, idx = lax.top_k(score, k_top)
    return idx, vals > -jnp.inf

def sparse_attend(q, ks, vs, valid):
    s = jnp.einsum('bthd,btkhd->bthk', q, ks).astype(jnp.float32) * HEAD_DIM ** -0.5
    s = jnp.where(valid[:, :, None, :], s, -jnp.inf)
    p = jax.nn.softmax(s, axis=-1).astype(vs.dtype)
    return jnp.einsum('bthk,btkhd->bthd', p, vs)

def gather_rows(rows, idx):
    return jax.vmap(lambda r, i: r[i])(rows, idx)

def prompt_attend(q, k, v, qi, ki, wi):
    bsz, seq = q.shape[:2]
    nb = seq // Q_BLOCK
    k_top = min(TOPK_MAX, seq // 4)

    def blocks(t):
        return t.reshape(bsz, nb, Q_BLOCK, *t.shape[2:]).swapaxes(0, 1)

    def one_block(args):
        i, qb, qib, wib = args
        q_pos = i * Q_BLOCK + jnp.arange(Q_BLOCK)
        idx, valid = index_select(qib, wib, ki, q_pos, k_top)
        return sparse_attend(qb, gather_rows(k, idx), gather_rows(v, idx), valid)

    out = lax.map(one_block, (jnp.arange(nb), blocks(q), blocks(qi), blocks(wi)))
    return out.swapaxes(0, 1).reshape(q.shape)

def make_sample_attend(cache_k, cache_v, cache_kidx, page_table, layer):
    def attend(q, k, v, qi, ki, wi):
        bsz, t_new = q.shape[:2]
        n_keys = PAST_LEN + t_new
        k_top = min(TOPK_MAX, n_keys // 4)
        ki_past = cache_kidx[page_table, layer].reshape(bsz, PAST_LEN, IDX_DIM)
        ki_all = jnp.concatenate([ki_past.astype(ki.dtype), ki], axis=1)
        idx, valid = index_select(qi, wi, ki_all, PAST_LEN + jnp.arange(t_new), k_top)
        in_past = idx < PAST_LEN
        pi = jnp.minimum(idx, PAST_LEN - 1)
        phys = jnp.take_along_axis(page_table, (pi // PAGE_SIZE).reshape(bsz, -1), axis=1).reshape(idx.shape)
        off = pi % PAGE_SIZE
        ni = jnp.clip(idx - PAST_LEN, 0, t_new - 1)

        def pick(cache, new):
            old = cache[phys, layer, off].astype(new.dtype)
            return jnp.where(in_past[..., None, None], old, gather_rows(new, ni))

        return sparse_attend(q, pick(cache_k, k), pick(cache_v, v), valid)
    return attend

def trunk_layer(x, params, l, pos, ssd_conv_prev, ssm_prev, cc_conv_prev, ffn_conv_prev, attend):
    bsz, t, _ = x.shape
    points = [int(c) for c in np.cumsum(IN_SIZES)[:-1]]
    u = x @ params['w_in'][l]
    z, xbc, dt_raw, q, k, v, qi, ki, wi, glu = jnp.split(u, points, axis=-1)
    xbc, ssd_conv_new = causal_dwconv(xbc, ssd_conv_prev, params['ssd_conv_w'][l], params['ssd_conv_b'][l])
    xbc = jax.nn.silu(xbc).astype(jnp.float32)
    gn = SSD_GROUPS * SSD_STATE
    xs = xbc[..., :SSD_INNER].reshape(bsz, t, SSD_HEADS, HEAD_DIM)
    bm = xbc[..., SSD_INNER:SSD_INNER + gn].reshape(bsz, t, SSD_GROUPS, SSD_STATE)
    cm = xbc[..., SSD_INNER + gn:].reshape(bsz, t, SSD_GROUPS, SSD_STATE)
    dt = jax.nn.softplus(dt_raw.astype(jnp.float32) + params['ssd_dt_bias'][l].astype(jnp.float32))
    a = -jnp.exp(params['ssd_a_log'][l].astype(jnp.float32))
    y_ssd, ssm_new = ssd_scan(xs, dt, a, bm, cm, ssm_prev.astype(jnp.float32))
    y_ssd = (y_ssd + params['ssd_d'][l].astype(jnp.float32)[:, None] * xs).reshape(bsz, t, SSD_INNER)
    y_ssd = rms_norm(y_ssd.astype(x.dtype) * jax.nn.silu(z), params['ssd_norm_g'][l])
    q = rope(q.reshape(bsz, t, ATT_HEADS, HEAD_DIM), pos)
    k = rope(k.reshape(bsz, t, ATT_HEADS, HEAD_DIM), pos)
    v = v.reshape(bsz, t, ATT_HEADS, HEAD_DIM)
    qi = rope(qi.reshape(bsz, t, IDX_HEADS, IDX_DIM), pos)
    ki = rope(ki.reshape(bsz, t, 1, IDX_DIM), pos)[:, :, 0]
    y_att = attend(q, k, v, qi, ki, wi).reshape(bsz, t, ATT_WIDTH)
    gl = glu[..., :CC_WIDTH] * jax.nn.sigmoid(glu[..., CC_WIDTH:])
    c, cc_conv_new = causal_dwconv(gl, cc_conv_prev, params['cc_conv_w'][l], params['cc_conv_b'][l])
    y_cc = jax.nn.silu(layer_norm(c, params['cc_ln_g'][l], params['cc_ln_b'][l]))
    mix = jnp.concatenate([y_ssd, y_att, y_cc], axis=-1) @ params['w_out'][l]
    x = layer_norm(ALPHA * x + mix, params['ln1_g'][l], params['ln1_b'][l])
    up = x @ params['ffn_w_up'][l]
    up, ffn_conv_new = causal_dwconv(up, ffn_conv_prev, params['ffn_conv_w'][l], params['ffn_conv_b'][l])
    f = (jax.nn.silu(up[..., D_FF:]) * up[..., :D_FF]) @ params['ffn_w_down'][l]
    x = layer_norm(ALPHA * x + f, params['ln2_g'][l], params['ln2_b'][l])
    return x, (k, v, ki, ssm_new.astype(x.dtype), ssd_conv_new, cc_conv_new, ffn_conv_new)

def setup_inputs(seed: int = 0) -> dict:
    key = jax.random.key(seed)
    keys = iter(jax.random.split(key, 48))
    f32 = jnp.float32

    def nrm(shape, scale):
        return jax.random.normal(next(keys), shape, f32) * scale

    n_pages = PAST_LEN // PAGE_SIZE
    n_used = DEC_BATCH * n_pages
    n_pool = n_used + (n_used + 3) // 4
    x_prompt = nrm((BATCH, SEQ, D_MODEL), 1.0)
    x_sample = nrm((DEC_BATCH, DEC_SEQ, D_MODEL), 1.0)
    cache_k = nrm((n_pool, DEPTH, PAGE_SIZE, ATT_HEADS, HEAD_DIM), 1.0)
    cache_v = nrm((n_pool, DEPTH, PAGE_SIZE, ATT_HEADS, HEAD_DIM), 1.0)
    cache_kidx = nrm((n_pool, DEPTH, PAGE_SIZE, IDX_DIM), 1.0)
    page_table = jax.random.permutation(next(keys), n_pool)[:n_used].reshape(DEC_BATCH, n_pages).astype(jnp.int32)
    state_ssm = nrm((DEC_BATCH, DEPTH, SSD_HEADS, HEAD_DIM, SSD_STATE), 0.5)
    state_ssd_conv = nrm((DEC_BATCH, DEPTH, SSD_CONV_W - 1, SSD_CONV_DIM), 1.0)
    state_cc_conv = nrm((DEC_BATCH, DEPTH, CC_CONV_W - 1, CC_WIDTH), 0.5)
    state_ffn_conv = nrm((DEC_BATCH, DEPTH, FFN_CONV_W - 1, 2 * D_FF), 1.0)
    dt0 = jnp.exp(jax.random.uniform(next(keys), (DEPTH, SSD_HEADS), f32, math.log(1e-3), math.log(1e-1)))
    ssd_dt_bias = dt0 + jnp.log(-jnp.expm1(-dt0))
    ssd_a_log = jnp.log(jax.random.uniform(next(keys), (DEPTH, SSD_HEADS), f32, 1.0, 16.0))
    return {
        'x_prompt': x_prompt, 'x_sample': x_sample,
        'cache_k': cache_k, 'cache_v': cache_v, 'cache_kidx': cache_kidx, 'page_table': page_table,
        'state_ssm': state_ssm, 'state_ssd_conv': state_ssd_conv,
        'state_cc_conv': state_cc_conv, 'state_ffn_conv': state_ffn_conv,
        'ln0_g': 1.0 + nrm((D_MODEL,), 0.02), 'ln0_b': nrm((D_MODEL,), 0.02),
        'w_in': nrm((DEPTH, D_MODEL, D_IN), D_MODEL ** -0.5),
        'ssd_conv_w': nrm((DEPTH, SSD_CONV_W, SSD_CONV_DIM), SSD_CONV_W ** -0.5),
        'ssd_conv_b': nrm((DEPTH, SSD_CONV_DIM), 0.02),
        'ssd_dt_bias': ssd_dt_bias, 'ssd_a_log': ssd_a_log,
        'ssd_d': 1.0 + nrm((DEPTH, SSD_HEADS), 0.02),
        'ssd_norm_g': 1.0 + nrm((DEPTH, SSD_INNER), 0.02),
        'cc_conv_w': nrm((DEPTH, CC_CONV_W, CC_WIDTH), CC_CONV_W ** -0.5),
        'cc_conv_b': nrm((DEPTH, CC_WIDTH), 0.02),
        'cc_ln_g': 1.0 + nrm((DEPTH, CC_WIDTH), 0.02), 'cc_ln_b': nrm((DEPTH, CC_WIDTH), 0.02),
        'w_out': nrm((DEPTH, MIX_WIDTH, D_MODEL), MIX_WIDTH ** -0.5 * BETA),
        'ln1_g': 1.0 + nrm((DEPTH, D_MODEL), 0.02), 'ln1_b': nrm((DEPTH, D_MODEL), 0.02),
        'ffn_w_up': nrm((DEPTH, D_MODEL, 2 * D_FF), D_MODEL ** -0.5),
        'ffn_conv_w': nrm((DEPTH, FFN_CONV_W, 2 * D_FF), FFN_CONV_W ** -0.5),
        'ffn_conv_b': nrm((DEPTH, 2 * D_FF), 0.02),
        'ffn_w_down': nrm((DEPTH, D_FF, D_MODEL), D_FF ** -0.5 * BETA),
        'ln2_g': 1.0 + nrm((DEPTH, D_MODEL), 0.02), 'ln2_b': nrm((DEPTH, D_MODEL), 0.02),
    }

def reference(x_prompt, x_sample, cache_k, cache_v, cache_kidx, page_table, state_ssm, state_ssd_conv,
              state_cc_conv, state_ffn_conv, ln0_g, ln0_b, w_in, ssd_conv_w, ssd_conv_b, ssd_dt_bias,
              ssd_a_log, ssd_d, ssd_norm_g, cc_conv_w, cc_conv_b, cc_ln_g, cc_ln_b, w_out, ln1_g, ln1_b,
              ffn_w_up, ffn_conv_w, ffn_conv_b, ffn_w_down, ln2_g, ln2_b):
    params = {'w_in': w_in, 'ssd_conv_w': ssd_conv_w, 'ssd_conv_b': ssd_conv_b, 'ssd_dt_bias': ssd_dt_bias,
              'ssd_a_log': ssd_a_log, 'ssd_d': ssd_d, 'ssd_norm_g': ssd_norm_g, 'cc_conv_w': cc_conv_w,
              'cc_conv_b': cc_conv_b, 'cc_ln_g': cc_ln_g, 'cc_ln_b': cc_ln_b, 'w_out': w_out,
              'ln1_g': ln1_g, 'ln1_b': ln1_b, 'ffn_w_up': ffn_w_up, 'ffn_conv_w': ffn_conv_w,
              'ffn_conv_b': ffn_conv_b, 'ffn_w_down': ffn_w_down, 'ln2_g': ln2_g, 'ln2_b': ln2_b}

    bp, sp = x_prompt.shape[:2]
    dtp = x_prompt.dtype
    h = layer_norm(x_prompt, ln0_g, ln0_b)
    pos_p = jnp.arange(sp)
    p_states = []
    for l in range(DEPTH):
        h, st = trunk_layer(h, params, l, pos_p,
                            jnp.zeros((bp, SSD_CONV_W - 1, SSD_CONV_DIM), dtp),
                            jnp.zeros((bp, SSD_HEADS, HEAD_DIM, SSD_STATE), dtp),
                            jnp.zeros((bp, CC_CONV_W - 1, CC_WIDTH), dtp),
                            jnp.zeros((bp, FFN_CONV_W - 1, 2 * D_FF), dtp),
                            prompt_attend)
        p_states.append(st)
    y_prompt = h

    ts = x_sample.shape[1]
    g = layer_norm(x_sample, ln0_g, ln0_b)
    pos_s = PAST_LEN + jnp.arange(ts)
    s_states = []
    for l in range(DEPTH):
        attend = make_sample_attend(cache_k, cache_v, cache_kidx, page_table, l)
        g, st = trunk_layer(g, params, l, pos_s, state_ssd_conv[:, l], state_ssm[:, l],
                            state_cc_conv[:, l], state_ffn_conv[:, l], attend)
        s_states.append(st)
    y_sample = g

    p_k, p_v, p_kidx, p_ssm, p_ssd_conv, p_cc_conv, p_ffn_conv = [jnp.stack(a, axis=1) for a in zip(*p_states)]
    s_k, s_v, s_kidx, s_ssm, s_ssd_conv, s_cc_conv, s_ffn_conv = [jnp.stack(a, axis=1) for a in zip(*s_states)]
    return (y_prompt, y_sample, p_k, p_v, p_kidx, p_ssm, p_ssd_conv, p_cc_conv, p_ffn_conv,
            s_k, s_v, s_kidx, s_ssm, s_ssd_conv, s_cc_conv, s_ffn_conv)


_drawn_inputs = setup_inputs


def setup_inputs(seed=0):
    import zlib

    import numpy as np

    out = dict(_drawn_inputs(seed))
    spreads = {}
    factors = {'cache_k': 2.845,
     'ssd_d': 8.0,
     'ssd_norm_g': 7.998,
     'cc_conv_b': 8.0,
     'cc_ln_g': 8.0,
     'cc_ln_b': 8.0,
     'ffn_conv_b': 6.35}
    for name, (base, spread) in spreads.items():
        noise = np.random.default_rng([zlib.crc32(name.encode()), seed]).standard_normal(out[name].shape)
        drawn = base * np.exp(spread * noise) if base else spread * noise
        out[name] = __import__('jax').numpy.asarray(drawn.astype(out[name].dtype))
    for name, factor in factors.items():
        out[name] = (out[name] * factor).astype(out[name].dtype)
    return out
```

```python
from contextlib import ExitStack

import numpy as np

import concourse.bass as bass
from concourse import mybir

F32 = mybir.dt.float32
I32 = mybir.dt.int32
ALU = mybir.AluOpType
ACT = mybir.ActivationFunctionType
AX = mybir.AxisListType

D_MODEL, SEQ, DEPTH, DEC_BATCH, DEC_SEQ, PAST_LEN, PAGE = 1024, 1024, 2, 8, 4, 2048, 128
HEAD, SSD_HEADS, SSD_STATE, SSD_W = 64, 8, 64, 4
SSD_INNER = SSD_HEADS * HEAD
SSD_CONV = SSD_INNER + 4 * SSD_STATE
ATT_HEADS, IDX_HEADS, TOPK = 4, 4, 256
CC_WIDTH, CC_W, D_FF, FFN_W = 256, 31, 2816, 3
ALPHA, EPS = (2 * DEPTH) ** 0.25, 1e-5
P = 128
NS = DEC_BATCH * DEC_SEQ
TOK = SEQ + NS
KT = D_MODEL // P
PAGES = PAST_LEN // PAGE
NCHUNK = SEQ // P
FF = D_FF // P
GROUPS = 2
FG = FF // GROUPS
SKEYS = PAST_LEN + NS
BIG = -1.0e30
TAKEN = -3.0e38
COLS = [(0, 512), (512, 512), (SEQ, NS)]

T_KI, T_QI, T_XBC, T_GATE, T_GLU, T_Z, T_K, T_Q, T_V = 0, 1, 3, 9, 11, 13, 17, 19, 21
N_IN = 23
DT_ROW, WI_ROW = 64, 96

_at = 0


def _cols(n):
    global _at
    _at += n
    return _at - n


V_SSDW, V_SSDB = _cols(6 * SSD_W), _cols(6)
V_CCW, V_CCB, V_CCG, V_CCBE = _cols(2 * CC_W), _cols(2), _cols(2), _cols(2)
V_RMSG, V_D = _cols(4), _cols(4)
V_LN1G, V_LN1B, V_LN2G, V_LN2B = _cols(KT), _cols(KT), _cols(KT), _cols(KT)
V_FFW, V_FFB = _cols(2 * FF * FFN_W), _cols(2 * FF)
V_ALOG, V_DTB = _cols(SSD_HEADS), _cols(1)
NVEC = _at

CONSTS = {}
_c = 0
for _n, _w in (("ident", P), ("causal", P), ("causalT", P), ("tri", P), ("rot", P), ("dup", P), ("rotdup", P), ("swap", P),
               ("causalT_s", NS), ("tri_s", NS), ("block_s", NS), ("newmask", NS), ("rep", P), ("repT", NS),
               ("hsel", IDX_HEADS), ("bsel", DEC_BATCH), ("cos", TOK), ("sin", TOK)):
    CONSTS[_n] = (_c, _w)
    _c += _w
NCONST = _c

def seg(width):
    h = width - 1
    return h, h + SEQ, h + DEC_SEQ, h + SEQ + DEC_BATCH * (h + DEC_SEQ)


SSD_H, SSD_S0, SSD_SEG, SSD_LEN = seg(SSD_W)
CC_H, CC_S0, CC_SEG, CC_LEN = seg(CC_W)
FFN_H, FFN_S0, FFN_SEG, FFN_LEN = seg(FFN_W)
SLOT = FG * P
NSLOT = 4
ROWS = DEC_BATCH * 16

JOBS = []
for _j in range(N_IN):
    JOBS.append(("in", _j))
    if _j == T_QI:
        JOBS += [("dup",), ("rotdup",), ("turn",)]
    if _j - 1 in (T_QI, T_QI + 1, T_K, T_K + 1, T_Q, T_Q + 1):
        JOBS.append(("rot", _j - 1))
N_A = len(JOBS)
JOBS += [("mean", "cc"), ("var", "cc"), ("var", "rms")]
JOBS += [("out", _j) for _j in range(KT)]
JOBS += [("mean", "ln1"), ("var", "ln1")]
for _g in range(GROUPS):
    JOBS += [("up", _g, _j) for _j in range(2 * FG)]
    JOBS += [("down", _g, _j) for _j in range(KT)]
JOBS += [("mean", "ln2"), ("var", "ln2")]
JOB = {name: n for n, name in enumerate(JOBS)}
JOB[("mean", "ln0")], JOB[("var", "ln0")] = 0, 1

LOADS = [("in", _j) for _j in range(N_IN)]
LOADS += [(_k, _g) for _k in ("kidx", "key", "value") for _g in range(DEC_BATCH * PAGES // 4)]
LOADS += [n for n in JOBS if n[0] in ("out", "up", "down")]
SLOTS, ARRIVED = {}, {}
_sum = [0] * NSLOT
for _n, _name in enumerate(LOADS):
    SLOTS[_name] = _n % NSLOT
    _sum[_n % NSLOT] += 64 if _name[0] in ("kidx", "key", "value") else 16
    ARRIVED[_name] = _sum[_n % NSLOT]

NORM_TILES = {"ln0": KT, "cc": 2, "rms": 4, "ln1": KT, "ln2": KT}
NORM_BASE = {"ln0": 0, "cc": 0, "rms": 2, "ln1": 6, "ln2": 6 + KT}
BLOCKS = [(i, h) for i in range(NCHUNK) for h in range(ATT_HEADS)]
SCORED = [(i, h) for i in range(2, NCHUNK) for h in range(IDX_HEADS)]
CHUNKS = [(c * P, P) for c in range(NCHUNK)] + [(SEQ, NS)]
STREAM = DEC_BATCH * PAGES // 4

NORM_SKIP = {"ln0": 0, "cc": 0, "rms": 1, "ln1": 2, "ln2": 3}
NORM_ORDER = {"ln0": 1, "cc": 1, "rms": 2, "ln1": 3, "ln2": 4}
IDX_SCALE, ATT_SCALE = HEAD ** -0.5, HEAD ** -0.5
WORK_SIZE = 26048

def build(nc, xT, w_in, w_out, w_up, w_down, vec, ln0, const, pages, cache_k, cache_v, cache_kidx,
          ssm_in, ssd_in, cc_in, ffn_in, yT, kT_out, v_out, ki_out, ssm_p, ssm_s, ssd_out, cc_out, ffn_out):
    ctx = ExitStack()
    with ctx:
        def sb(name, shape, dt=F32):
            return ctx.enter_context(nc.sbuf_tensor(name, shape, dt))

        def sem(name):
            return ctx.enter_context(nc.semaphore(name))

        X = sb("X", [P, KT, TOK])
        MIX = sb("MIX", [P, KT, TOK])
        VEC = sb("VEC", [P, NVEC])
        LN0 = sb("LN0", [P, 2 * KT])
        CONST = sb("CONST", [P, NCONST])
        PT = sb("PT", [1, DEC_BATCH * PAGES], I32)
        ONES = sb("ONES", [P, P])
        MEAN = {256: sb("MEAN256", [P, P]), 512: sb("MEAN512", [P, P]), 1024: sb("MEAN1024", [P, P])}
        EPSC = sb("EPSC", [P, 1])
        EXPA = sb("EXPA", [P, SSD_HEADS])
        RING = sb("RING", [P, NSLOT, SLOT])
        WORK = sb("WORK", [P, WORK_SIZE])
        PS = ctx.enter_context(nc.psum_tensor("PS", [P, 8 * 512], F32))

        def c(name, rows=P):
            at, w = CONSTS[name]
            return CONST[0:rows, at:at + w]

        def v(col, rows=slice(0, P)):
            return VEC[rows, col:col + 1]

        at = [0]

        def view(*dims):
            n = int(np.prod(dims))
            a = WORK[:, at[0]:at[0] + n]
            at[0] += n
            assert at[0] <= WORK_SIZE, at[0]
            if len(dims) == 2:
                return a.rearrange("p (a b) -> p a b", a=dims[0])
            if len(dims) == 3:
                return a.rearrange("p (a b c) -> p a b c", a=dims[0], b=dims[1])
            return a

        QT = view(2, TOK)
        KTL = view(2, TOK)
        VTOK = view(NCHUNK + 1, 256)
        DTT = view(NCHUNK + 1, SSD_HEADS)
        WIT = view(NCHUNK + 1, IDX_HEADS)
        qi_at = at[0]
        QI = view(2, TOK)
        KID = view(TOK)
        common = at[0]
        SEL_AT, n_sel = {}, 0
        for i in range(2, NCHUNK):
            SEL_AT[i] = n_sel
            n_sel += (i + 1) * P
        SEL = view(n_sel)
        SELS = view(SKEYS)
        xbc_at = at[0]
        XBC = view(6, SSD_LEN)
        rest = at[0]
        at[0] = common
        T0 = view(TOK)
        CC = view(2, CC_LEN)
        SSDH, CCH = view(6, DEC_BATCH * SSD_H), view(2, DEC_BATCH * CC_H)
        SSDO, CCO = view(6, SSD_H * (1 + DEC_BATCH)), view(2, CC_H * (1 + DEC_BATCH))
        ROPE = view(TOK)
        assert at[0] <= xbc_at
        at[0] = rest
        ACC = view(2, CC_LEN)
        at[0] = rest
        RELU = view(SKEYS)
        KXT = view(2, 512)
        QIS = MIX[:, 4:6, :].rearrange("p a b -> p (a b)")[:, 0:DEC_BATCH * (P + 16)]
        WMAT = MIX[:, 5, 512:512 + NS]
        WCOL = MIX[:, 5, 600:610]
        at[0] = qi_at
        BTOK = view(P)
        DA, CUM, WS, T8 = view(SSD_HEADS), view(SSD_HEADS), view(SSD_HEADS), view(8)
        XDT, XW = view(SSD_HEADS, HEAD), view(SSD_HEADS, HEAD)
        E2, CE, YT = view(4, P), view(4, P), view(4, P)
        assert at[0] <= common
        at[0] = rest
        DEC = view(SSD_HEADS, P)
        HP = view(4, HEAD)
        HS = view(DEC_BATCH, 4, HEAD)
        XWB = DEC.rearrange("p a b -> p (a b)").rearrange("p (a b) -> p a b", a=2)
        at[0] = xbc_at
        SC = view(2, SEQ)
        PROBT = view(2, SEQ)
        NMAX, RSUM = view(len(BLOCKS)), view(len(BLOCKS))
        at[0] = xbc_at
        KQ = view(DEC_BATCH * (2 * P + 16))
        KTS = view(2, 1024)
        PR = view(SKEYS)
        PRT = view(PAGES + 1, P)
        SMAX, SSUM = view(1), view(1)
        at[0] = 0
        HID = view(FG, TOK)
        U = view(2, FFN_LEN)
        FACC = view(2, FFN_LEN)
        GATE = view(FFN_LEN)
        FFH, FFO = view(2 * FF, DEC_BATCH * FFN_H), view(2 * FF, FFN_H * (1 + DEC_BATCH))
        assert at[0] <= WORK_SIZE - 3 * TOK
        at[0] = WORK_SIZE - 3 * TOK
        SQ_TOP, RSTD_TOP = view(2, TOK), view(TOK)

        def ring(name):
            return RING[:, SLOTS[name], :]

        def cache_page(name):
            return ring(name)[:, 0:1024].rearrange("p (j n) -> p j n", j=4)

        const_loaded, set_up, cleared, engines_done, acked = (sem(n) for n in (
            "const_loaded", "set_up", "cleared", "engines_done", "acked"))
        stage_done = sem("stage_done")
        full = [sem("bank_set_full0"), sem("bank_set_full1")]
        free = [sem("bank_set_free0"), sem("bank_set_free1")]
        loaded = [sem(f"slot_loaded{s}") for s in range(NSLOT)]
        vec_loaded, hist_loaded, stored = sem("vec_loaded"), sem("hist_loaded"), sem("stored")
        vector_step, scalar_step, pool_step = sem("vector_step"), sem("scalar_step"), sem("pool_step")
        hist_set, saved, conv_done, silu_done, cc_ready = (sem(n) for n in (
            "history_set", "states_saved", "conv_done", "silu_done", "cc_ready"))
        soft_v, soft_a = sem("softplus_by_vector"), sem("softplus_by_scalar")
        ln_ready, ln_sq, ln_used, ln_std, ln_mul, ln_out = (sem(n) for n in (
            "norm_ready", "norm_squared", "norm_squares_used", "norm_rstd", "norm_scaled", "norm_out"))
        idx_full, idx_relu, idx_added = sem("index_products"), sem("index_relu"), sem("index_added")
        tr_full, tr_copied, tr_used = sem("pages_turned"), sem("pages_copied"), sem("pages_used")
        v_used = sem("values_used")
        ssd = {n: sem("ssd_" + n) for n in ("turned", "taken", "sums", "seg", "decay", "weighed", "y", "h",
                                            "state", "masked")}
        att = {n: sem("att_" + n) for n in ("scores", "masked", "exp", "normed", "turned", "copied", "out",
                                            "out_read")}
        smp = {n: sem("sample_" + n) for n in ("swap", "q", "w", "wmat", "products", "relu", "scores", "selected", "kq",
                                               "logits", "max", "exp", "normed", "turned", "copied", "out")}
        u_hist, u_conv, gate_done, hid_done, ffn_saved = (sem(n) for n in (
            "up_history", "up_convolved", "gate_done", "hidden_done", "ffn_state_saved"))
        layer_sems = range(stage_done.num, ffn_saved.num + 1)

        block = ctx.enter_context(nc.Block())

        class Steps:
            def __init__(self, eng, s):
                self.eng, self.sem, self.n = eng, s, 0

            def then_wait(self, ins):
                ins.then_inc(self.sem, 1)
                self.n += 1
                self.eng.wait_ge(self.sem, self.n)

        class Stages:
            def __init__(self, eng):
                self.eng, self.n = eng, 0

            def end(self):
                self.n += 1
                self.eng.drain().then_inc(stage_done, 1)
                self.eng.wait_ge(stage_done, 4 * self.n)

        def between_layers(eng):
            eng.drain().then_inc(engines_done, 1)
            eng.wait_ge(cleared, 1)
            eng.drain().then_inc(acked, 1)

        def bank(b, n=512, rows=slice(0, P)):
            return PS[rows, 512 * b:512 * b + n]

        def job_psum(n, w=TOK, rows=slice(0, P), first=0):
            b = 3 * (n % 2) * 512 + first
            return PS[rows, b:b + w]

        def await_full(eng, n):
            eng.wait_ge(full[n % 2], n // 2 + 1)

        def await_freed(eng, n):
            eng.wait_ge(free[n % 2], n // 2 + 1)

        def samples(a, seg_len, first, n):
            return a.rearrange("p (b s) -> p b s", s=seg_len)[:, :, first:first + n]

        def by_sample(a, n=DEC_SEQ):
            return a.rearrange("p (b t) -> p b t", t=n)

        def norm_source(name):
            return {"cc": (MIX, 6), "rms": (MIX, 0), "ln0": (X, 0), "ln1": (X, 0), "ln2": (MIX, 0)}[name]

        def norm_src(name, k):
            t, first = norm_source(name)
            return t[:, first + k, :]

        def norm_tmp(name):
            if name == "cc":
                return [MIX[:, 4, :], MIX[:, 5, :]], CC[:, 0, 0:TOK]
            if name == "rms":
                return [MIX[:, 4, :], MIX[:, 5, :]], WORK[:, qi_at:qi_at + TOK]
            return [SQ_TOP[:, 0, :], SQ_TOP[:, 1, :]], RSTD_TOP

        def norm_width(name):
            return MEAN[{"cc": CC_WIDTH, "rms": SSD_INNER}.get(name, D_MODEL)]

        @block.sync
        def _(sp):
            for dst, src in ((CONST[:, :], const), (X[:, :, :], xT), (LN0[:, :], ln0), (PT[:, :], pages)):
                sp.dma_start(dst, src).then_inc(const_loaded, 16)
            sp.wait_ge(const_loaded, 64)

            with sp.Fori(0, DEPTH) as layer:
                sp.wait_ge(engines_done, 4)
                sp.drain()
                sp.sem_clear(layer_sems)
                sp.sem_clear(engines_done)
                sp.drain().then_inc(cleared, 1)
                sp.wait_ge(acked, 4)
                sp.drain()
                sp.sem_clear(acked)
                sp.sem_clear(cleared)

                def store(dst, src):
                    sp.dma_start(dst, src).then_inc(stored, 16)

                sp.dma_start(VEC[:, :], vec[layer, :, :]).then_inc(vec_loaded, 16)
                sp.dma_start(SSDH[:, :, :], ssd_in[layer, :, :, :]).then_inc(hist_loaded, 16)
                sp.dma_start(CCH[:, :, :], cc_in[layer, :, :, :]).then_inc(hist_loaded, 16)
                for n, name in enumerate(LOADS):
                    kind, slot = name[0], n % NSLOT
                    if name == ("kidx", 0):
                        sp.wait_ge(saved, 8)
                        store(ssd_out[layer, :, :, :], SSDO[:, :, :])
                        store(cc_out[layer, :, :, :], CCO[:, :, :])
                        sp.wait_ge(stage_done, 4 * 1)
                        for t in range(2):
                            store(kT_out[layer, t, :, :], KTL[:, t, :])
                        store(v_out[layer, 0:P, 0:NCHUNK, :], VTOK[:, 0:NCHUNK, :])
                        store(v_out[layer, 0:NS, NCHUNK, :], VTOK[0:NS, NCHUNK, :])
                        store(ki_out[layer, :, :], KID[0:HEAD, :])
                    elif name == ("key", NSLOT):
                        sp.wait_ge(stage_done, 4 * 2)
                        sp.dma_start(HS[:, :, :, :], ssm_in[layer, :, :, :, :]).then_inc(hist_loaded, 16)
                        sp.wait_ge(ssd["state"], NCHUNK)
                        store(ssm_p[layer, :, :, :], HP[:, :, :])
                        sp.wait_ge(ssd["state"], NCHUNK + 1)
                        store(ssm_s[layer, :, :, :, :], HS[:, :, :, :])
                    if name == ("out", 0):
                        sp.wait_ge(stage_done, 4 * 5)
                        sp.dma_start(FFH[:, :, :], ffn_in[layer, :, :, :]).then_inc(hist_loaded, 16)
                    elif n >= NSLOT:
                        old = LOADS[n - NSLOT]
                        if old[0] in ("in", "out", "up", "down"):
                            await_full(sp, JOB[old])
                        elif old[0] == "value":
                            sp.wait_ge(v_used, old[1] + 1)
                        else:
                            sp.wait_ge(tr_full, old[1] + 1 + (STREAM if old[0] == "key" else 0))
                    if kind in ("kidx", "key", "value"):
                        cache = {"kidx": cache_kidx, "key": cache_k, "value": cache_v}[kind]
                        w = HEAD if kind == "kidx" else 256
                        for j in range(4):
                            k = 4 * name[1] + j
                            page = sp.value_load(PT[0:1, k:k + 1], min_val=0, max_val=cache_k.shape[0] - 1)
                            sp.dma_start(RING[:, slot, j * w:(j + 1) * w], cache[page, layer, :, :]
                                         ).then_inc(loaded[slot], 16)
                    elif kind == "in":
                        sp.dma_start(RING[:, slot, 0:KT * P], w_in[layer, name[1], :, :]).then_inc(loaded[slot], 16)
                    elif kind == "out":
                        sp.dma_start(RING[:, slot, 0:KT * P], w_out[layer, name[1], :, :]).then_inc(loaded[slot], 16)
                    elif kind == "up":
                        sp.dma_start(RING[:, slot, 0:KT * P], w_up[layer, name[1] * 2 * FG + name[2], :, :]
                                     ).then_inc(loaded[slot], 16)
                    else:
                        sp.dma_start(RING[:, slot, :], w_down[layer, name[1] * KT + name[2], :, :]
                                     ).then_inc(loaded[slot], 16)
                sp.wait_ge(ffn_saved, 2 * FF)
                store(ffn_out[layer, :, :, :], FFO[:, :, :])
                sp.wait_ge(stage_done, 4 * 7)
                store(yT, X[:, :, :])
                sp.wait_ge(stored, 16 * 11)

        @block.gpsimd
        def _(pool):
            pool.memset(ONES[:, :], 1.0)
            for n, t in MEAN.items():
                pool.memset(t[:, :], 1.0 / n)
            pool.memset(EPSC[:, :], EPS)
            pool.drain().then_inc(set_up, 1)
            pool.wait_ge(const_loaded, 64)

            with pool.Fori(0, DEPTH) as layer:
                between_layers(pool)
                stage = Stages(pool)
                pool.wait_ge(hist_loaded, 32)
                for t in range(6):
                    pool.memset(XBC[:, t, 0:SSD_H], 0.0)
                    pool.tensor_copy(samples(XBC[:, t, SSD_S0:], SSD_SEG, 0, SSD_H), by_sample(SSDH[:, t, :], SSD_H))
                for t in range(2):
                    pool.memset(CC[:, t, 0:CC_H], 0.0)
                    pool.tensor_copy(samples(CC[:, t, CC_S0:], CC_SEG, 0, CC_H), by_sample(CCH[:, t, :], CC_H))
                pool.drain().then_inc(hist_set, 1)
                for t in range(6):
                    await_freed(pool, JOB[("in", T_XBC + t)])
                    pool.tensor_copy(SSDO[:, t, 0:SSD_H], XBC[:, t, SEQ:SEQ + SSD_H])
                    pool.tensor_copy(by_sample(SSDO[:, t, SSD_H:], SSD_H),
                                     samples(XBC[:, t, SSD_S0:], SSD_SEG, DEC_SEQ, SSD_H)).then_inc(saved, 1)
                for t in range(2):
                    await_freed(pool, JOB[("in", T_GLU + t)])
                    pool.tensor_copy(CCO[:, t, 0:CC_H], CC[:, t, SEQ:SEQ + CC_H])
                    pool.tensor_copy(by_sample(CCO[:, t, CC_H:], CC_H),
                                     samples(CC[:, t, CC_S0:], CC_SEG, DEC_SEQ, CC_H)).then_inc(saved, 1)
                pool.wait_ge(stored, 16 * 2)
                stage.end()
                pool.memset(QIS, 0.0).then_inc(pool_step, 1)
                pool.wait_ge(stored, 16 * 7)
                stage.end()
                pool.memset(HP[:, :, :], 0.0).then_inc(pool_step, 1)
                pool.wait_ge(stored, 16 * 9)
                stage.end()
                stage.end()
                pool.memset(KQ, 0.0).then_inc(pool_step, 1)
                stage.end()
                for b in range(2):
                    pool.memset(U[:, b, 0:FFN_H], 0.0)
                pool.wait_ge(hist_loaded, 64)
                stage.end()
                for n in range(2 * FF):
                    g, j = divmod(n, 2 * FG)
                    if n >= 2:
                        pool.wait_ge(u_conv, n - 1)
                        pool.wait_ge(ffn_saved, n - 1)
                    pool.tensor_copy(samples(U[:, n % 2, FFN_S0:], FFN_SEG, 0, FFN_H),
                                     by_sample(FFH[:, n, :], FFN_H)).then_inc(u_hist, 1)
                    if n >= 1:
                        m = n - 1
                        await_freed(pool, JOB[("up", *divmod(m, 2 * FG))])
                        pool.tensor_copy(FFO[:, m, 0:FFN_H], U[:, m % 2, SEQ:SEQ + FFN_H])
                        pool.tensor_copy(by_sample(FFO[:, m, FFN_H:], FFN_H),
                                         samples(U[:, m % 2, FFN_S0:], FFN_SEG, DEC_SEQ, FFN_H)).then_inc(ffn_saved, 1)
                m = 2 * FF - 1
                await_freed(pool, JOB[("up", GROUPS - 1, 2 * FG - 1)])
                pool.tensor_copy(FFO[:, m, 0:FFN_H], U[:, m % 2, SEQ:SEQ + FFN_H])
                pool.tensor_copy(by_sample(FFO[:, m, FFN_H:], FFN_H),
                                 samples(U[:, m % 2, FFN_S0:], FFN_SEG, DEC_SEQ, FFN_H)).then_inc(ffn_saved, 1)
                pool.wait_ge(ffn_saved, 2 * FF)
                stage.end()
                pool.wait_ge(stored, 16 * 11)

        @block.tensor
        def _(pe):
            def product(n, stationary, moving, k_tiles):
                if n >= 2:
                    await_freed(pe, n - 2)
                for first, w in COLS:
                    for k in range(k_tiles):
                        mm = pe.matmul(job_psum(n, w, first=first), stationary(k), moving(k)[:, first:first + w],
                                       start=k == 0, stop=k == k_tiles - 1)
                mm.then_inc(full[n % 2], 1)

            def weights(name):
                pe.wait_ge(loaded[SLOTS[name]], ARRIVED[name])
                return ring(name).rearrange("p (k m) -> p k m", m=P)

            def norm(name):
                tiles, base = NORM_TILES[name], NORM_BASE[name]
                if ("mean", name) in JOB:
                    n = JOB[("mean", name)]
                    if name == "cc":
                        pe.wait_ge(cc_ready, 2)
                    elif name == "ln1":
                        await_freed(pe, JOB[("out", KT - 1)])
                        await_freed(pe, JOB[("out", KT - 2)])
                    elif name == "ln2":
                        await_freed(pe, JOB[("down", GROUPS - 1, KT - 1)])
                        await_freed(pe, JOB[("down", GROUPS - 1, KT - 2)])
                    product(n, lambda k: norm_width(name)[:, :], lambda k: norm_src(name, k), tiles)
                n = JOB[("var", name)]
                if n >= 2:
                    await_freed(pe, n - 2)
                squares = norm_tmp(name)[0]
                for k in range(tiles):
                    pe.wait_ge(ln_sq, base + k + 1)
                    for first, w in COLS:
                        mm = pe.matmul(job_psum(n, w, first=first), norm_width(name)[:, :],
                                       squares[k % 2][:, first:first + w], start=k == 0, stop=k == tiles - 1)
                    mm.then_inc(full[n % 2] if k == tiles - 1 else ln_used, 1)

            pe.wait_ge(const_loaded, 64)
            pe.wait_ge(set_up, 1)
            norm("ln0")
            with pe.Fori(0, DEPTH) as layer:
                between_layers(pe)
                stage = Stages(pe)

                for n in range(N_A):
                    name = JOBS[n]
                    if name[0] == "in" and name[1] < T_V:
                        w = weights(name)
                        product(n, lambda k: w[:, k, :], lambda k: X[:, k, :], KT)
                    elif name[0] == "in":
                        w = weights(name)
                        await_freed(pe, n - 2)
                        for ch, (first, length) in enumerate(CHUNKS):
                            for k in range(KT):
                                mm = pe.matmul(job_psum(n, P, slice(0, length), first=ch * P),
                                               X[:, k, first:first + length], w[:, k, :],
                                               start=k == 0, stop=k == KT - 1)
                        mm.then_inc(full[n % 2], 1)
                    elif name[0] in ("dup", "rotdup"):
                        await_freed(pe, JOB[("in", T_KI)])
                        product(n, lambda k: c(name[0], HEAD), lambda k: T0[0:HEAD, :], 1)
                    elif name[0] == "turn":
                        pe.wait_ge(soft_v, 4)
                        await_freed(pe, n - 2)
                        for ch, (first, length) in enumerate(CHUNKS):
                            mm = pe.transpose(job_psum(n, P, slice(0, length), first=ch * P),
                                              T0[:, first:first + length], c("ident"))
                        mm.then_inc(full[n % 2], 1)
                    else:
                        r = name[1]
                        await_freed(pe, JOB[("in", r)])
                        src = (QI[:, r - T_QI, :] if r < T_XBC else KTL[:, r - T_K, :] if r < T_Q
                               else QT[:, r - T_Q, :])
                        product(n, lambda k: c("rot"), lambda k: src, 1)
                norm("cc")
                stage.end()

                for n, (i, h) in enumerate(SCORED):
                    if n >= 2:
                        pe.wait_ge(idx_relu, n - 1)
                    keys, r = (i + 1) * P, (h % 2) * HEAD
                    for k in range(0, keys, 512):
                        w = min(512, keys - k)
                        mm = pe.matmul(bank(2 * (n % 2) + k // 512, w), QI[r:r + HEAD, h // 2, i * P:(i + 1) * P],
                                       KID[r:r + HEAD, k:k + w], start=True, stop=True)
                    mm.then_inc(idx_full, 1)
                for t in range(2):
                    mm = pe.matmul(bank(7)[:, 64 * t:64 * t + NS], c("swap"), QI[:, t, SEQ:TOK], start=True, stop=True)
                mm.then_inc(smp["swap"], 1)
                mm = pe.matmul(bank(7)[:, 256:256 + IDX_HEADS], c("rep", NS), WIT[0:NS, NCHUNK, :], start=True, stop=True)
                mm.then_inc(smp["swap"], 1)
                pe.wait_ge(smp["q"], 1)
                pe.wait_ge(idx_relu, len(SCORED))

                def turn_index(g):
                    name = ("kidx", g)
                    pe.wait_ge(loaded[SLOTS[name]], ARRIVED[name])
                    if g >= 2:
                        pe.wait_ge(tr_copied, g - 1)
                    for pair in range(2):
                        mm = pe.transpose(bank(5 + g % 2)[:, pair * P:(pair + 1) * P],
                                          ring(name)[:, pair * P:(pair + 1) * P], c("ident"))
                    mm.then_inc(tr_full, 1)

                turn_index(0)
                for g in range(STREAM):
                    if g + 1 < STREAM:
                        turn_index(g + 1)
                    b, q = divmod(g, PAGES // 4)
                    pe.wait_ge(tr_copied, g + 1)
                    for odd in range(2):
                        r = slice(HEAD * odd, HEAD * odd + HEAD)
                        mm = pe.matmul(bank(q // 2 * 2 + odd)[:, (q % 2) * 256:(q % 2) * 256 + 256],
                                       QIS[r, b * P:(b + 1) * P], KXT[r, g % 2, 0:256],
                                       start=b == 0 and q % 2 == 0, stop=b == DEC_BATCH - 1, skip_group_check=True)
                    mm.then_inc(tr_used, 1)
                for b in range(DEC_BATCH):
                    mm = pe.matmul(bank(4, NS), QIS[0:HEAD, b * P:(b + 1) * P], KID[0:HEAD, SEQ:TOK],
                                   start=b == 0, stop=b == DEC_BATCH - 1)
                mm.then_inc(smp["products"], 1)
                pe.wait_ge(smp["relu"], 1)
                pe.wait_ge(smp["wmat"], 1)
                for k in range(0, SKEYS, 512):
                    w = min(512, SKEYS - k)
                    mm = pe.matmul(bank(k // 512, w, slice(0, NS)), WMAT, RELU[:, k:k + w], start=True, stop=True)
                mm.then_inc(smp["scores"], 1)
                stage.end()

                for ch, (first, L) in enumerate(CHUNKS):
                    cols, rows = slice(first, first + L), slice(0, L)
                    last = ch == NCHUNK
                    if ch:
                        pe.wait_ge(ssd["taken"], ch)
                        pe.wait_ge(ssd["weighed"], ch)
                    for t in range(4):
                        pe.transpose(bank(0, rows=rows)[:, t * P:(t + 1) * P], XBC[:, t, cols], c("ident"))
                    pe.transpose(bank(1, P, rows), XBC[:, 4, cols], c("ident")).then_inc(ssd["turned"], 1)
                    pe.wait_ge(ssd["taken"], ch + 1)
                    tri = c("tri_s", L)[:, 0:L] if last else c("tri")
                    total = c("block_s", L)[:, 0:L] if last else ONES[:, :]
                    pe.matmul(bank(2, 8, rows), tri, DA[rows, :], start=True, stop=True)
                    pe.matmul(bank(2, 512, rows)[:, 8:16], total, DA[rows, :], start=True, stop=True)
                    for g in range(2):
                        r = slice(g * SSD_STATE, (g + 1) * SSD_STATE)
                        pe.matmul(bank(2 + 5 * g, 512, rows)[:, 256:256 + L], XBC[r, 4, cols], XBC[r, 5, cols],
                                  start=True, stop=True)
                    for h in range(SSD_HEADS):
                        pe.matmul(bank(3 + h // 4, 512, rows)[:, (h % 4) * P:(h % 4) * P + L],
                                  DA[rows, h:h + 1].broadcast_to([L, L]), tri, start=True, stop=True)
                    for h in range(SSD_HEADS):
                        r = slice((h // 4) * 64, (h // 4) * 64 + 64)
                        mm = pe.matmul(bank(5, 512, r)[:, (h % 4) * P:(h % 4) * P + L],
                                       DA[rows, h:h + 1].broadcast_to([L, 64]), tri, start=True, stop=True)
                    mm.then_inc(ssd["sums"], 1)
                    pe.wait_ge(ssd["weighed"], ch + 1)
                    if ch == 0:
                        pe.wait_ge(pool_step, 2)
                    if last:
                        pe.wait_ge(hist_loaded, 48)
                    for h in range(SSD_HEADS):
                        r, g, j = slice((h % 2) * 64, (h % 2) * 64 + 64), h // 4, h % 4
                        gr = slice(g * 64, g * 64 + 64)
                        y = bank(6 - g, 512, r)[:, (j // 2) * P:(j // 2) * P + L]
                        pe.matmul(y, XDT[rows, h, :], DEC[rows, h, 0:L], start=True, stop=False, skip_group_check=True)
                        if not last:
                            mm = pe.matmul(y, HP[gr, j, :], CE[gr, j, 0:L], start=False, stop=True,
                                           skip_group_check=True)
                        else:
                            for b in range(DEC_BATCH):
                                mm = pe.matmul(y[:, b * DEC_SEQ:(b + 1) * DEC_SEQ], HS[gr, b, j, :],
                                               CE[gr, j, b * DEC_SEQ:(b + 1) * DEC_SEQ],
                                               start=False, stop=b == DEC_BATCH - 1, skip_group_check=True)
                    mm.then_inc(ssd["y"], 1)
                    if not last:
                        for g in range(2):
                            gr = slice(g * 64, g * 64 + 64)
                            mm = pe.matmul(bank(7, 256, gr), BTOK[:, gr], XW[:, 4 * g:4 * g + 4, :],
                                           start=True, stop=True)
                        mm.then_inc(ssd["h"], 1)
                    else:
                        for b in range(DEC_BATCH):
                            pe.wait_ge(ssd["masked"], b + 1)
                            for g in range(2):
                                gr = slice(g * 64, g * 64 + 64)
                                mm = pe.matmul(bank(2 + b // 2, 512, gr)[:, (b % 2) * 256:(b % 2) * 256 + 256],
                                               BTOK[rows, gr], XWB[rows, b % 2, g * 256:(g + 1) * 256],
                                               start=True, stop=True)
                            mm.then_inc(ssd["h"], 1)
                norm("rms")
                stage.end()

                def scores(n):
                    i, h = BLOCKS[n]
                    if n >= 2:
                        pe.wait_ge(att["masked"], n - 1)
                    keys, r = (i + 1) * P, (h % 2) * HEAD
                    for k in range(0, keys, 512):
                        w = min(512, keys - k)
                        mm = pe.matmul(bank(2 * (n % 2) + k // 512, w), QT[r:r + HEAD, h // 2, i * P:(i + 1) * P],
                                       KTL[r:r + HEAD, h // 2, k:k + w], start=True, stop=True)
                    mm.then_inc(att["scores"], 1)

                def turn(n):
                    i, h = BLOCKS[n]
                    pe.wait_ge(att["normed"], n + 1)
                    if n >= 1:
                        pe.wait_ge(att["copied"], n)
                    for s in range(i + 1):
                        mm = pe.transpose(bank(4 + s // 4)[:, (s % 4) * P:(s % 4 + 1) * P],
                                          SC[:, n % 2, s * P:(s + 1) * P], c("ident"))
                    mm.then_inc(att["turned"], 1)

                def weigh(n):
                    i, h = BLOCKS[n]
                    pe.wait_ge(att["copied"], n + 1)
                    if h == 0 and i >= 1:
                        pe.wait_ge(att["out_read"], i)
                    r = slice((h % 2) * 64, (h % 2) * 64 + 64)
                    for s in range(i + 1):
                        mm = pe.matmul(bank(6 + h // 2, P, r), VTOK[:, s, h * HEAD:(h + 1) * HEAD],
                                       PROBT[:, n % 2, s * P:(s + 1) * P], start=s == 0, stop=s == i)
                    mm.then_inc(att["out"], 1)

                for n in range(len(BLOCKS) + 2):
                    if n < len(BLOCKS):
                        scores(n)
                    if 1 <= n <= len(BLOCKS):
                        turn(n - 1)
                    if n >= 2:
                        weigh(n - 2)
                stage.end()

                pe.wait_ge(smp["kq"], 1)

                def turn_keys(g):
                    name = ("key", g)
                    pe.wait_ge(loaded[SLOTS[name]], ARRIVED[name])
                    if g >= 1:
                        pe.wait_ge(tr_copied, STREAM + g)
                    for j in range(4):
                        for t in range(2):
                            mm = pe.transpose(bank(5 + t)[:, j * P:(j + 1) * P],
                                              cache_page(name)[:, j, t * P:(t + 1) * P], c("ident"))
                    mm.then_inc(tr_full, 1)

                def score_keys(g):
                    b, q = divmod(g, PAGES // 4)
                    pe.wait_ge(tr_copied, STREAM + g + 1)
                    for t in range(2):
                        mm = pe.matmul(bank(q), KQ[:, b * 256 + t * P:b * 256 + (t + 1) * P],
                                       KTS[:, g % 2, t * 512:(t + 1) * 512], start=b == 0 and t == 0, stop=False,
                                       skip_group_check=True)
                    mm.then_inc(tr_used, 1)

                for g in range(STREAM + 1):
                    if g < STREAM:
                        turn_keys(g)
                    if g >= 1:
                        score_keys(g - 1)
                for b in range(DEC_BATCH):
                    for t in range(2):
                        pe.matmul(bank(4, NS), KQ[:, b * 256 + t * P:b * 256 + (t + 1) * P], KTL[:, t, SEQ:TOK],
                                  start=b == 0 and t == 0, stop=False, skip_group_check=True)
                for k in range(0, SKEYS, 512):
                    w = min(512, SKEYS - k)
                    mm = pe.matmul(bank(k // 512, w), c("rep", NS), SELS[0:NS, k:k + w], start=False, stop=True,
                                   skip_group_check=True)
                mm.then_inc(smp["logits"], 1)
                pe.wait_ge(smp["normed"], 1)
                for s in range(PAGES + 1):
                    w = P if s < PAGES else NS
                    mm = pe.transpose(bank(s // 4, 512, slice(0, w))[:, (s % 4) * P:(s % 4 + 1) * P],
                                      PR[:, s * P:s * P + w], c("ident"))
                mm.then_inc(smp["turned"], 1)
                pe.wait_ge(smp["copied"], 2)
                for t in range(2):
                    pe.matmul(bank(7)[:, t * P:(t + 1) * P], VTOK[0:NS, NCHUNK, t * P:(t + 1) * P],
                              PRT[0:NS, PAGES, :], start=t == 0, stop=False, skip_group_check=True)
                for g in range(STREAM):
                    b, q = divmod(g, PAGES // 4)
                    name = ("value", g)
                    pe.wait_ge(loaded[SLOTS[name]], ARRIVED[name])
                    for j in range(4):
                        for t in range(2):
                            mm = pe.matmul(bank(7)[:, t * P + 16 * b:t * P + 16 * b + 16],
                                           cache_page(name)[:, j, t * P:(t + 1) * P],
                                           PRT[:, 4 * q + j, 16 * b:16 * b + 16], start=False,
                                           stop=g == STREAM - 1 and j == 3, skip_group_check=True)
                    mm.then_inc(v_used, 1)
                stage.end()

                for j in range(KT):
                    w = weights(("out", j))
                    product(JOB[("out", j)], lambda k: w[:, k, :], lambda k: MIX[:, k, :], KT)
                norm("ln1")
                stage.end()
                for g in range(GROUPS):
                    for j in range(2 * FG):
                        w = weights(("up", g, j))
                        product(JOB[("up", g, j)], lambda k: w[:, k, :], lambda k: X[:, k, :], KT)
                    pe.wait_ge(hid_done, FG * (g + 1))
                    for j in range(KT):
                        w = weights(("down", g, j))
                        product(JOB[("down", g, j)], lambda k: w[:, k, :], lambda k: HID[:, k, :], FG)
                norm("ln2")
                stage.end()

        @block.scalar
        def _(act):
            def copy(dst, src):
                return act.activation(dst, src, ACT.Copy)

            def norm(name, func, gcol, bcol, dst, params=VEC):
                tiles, base = NORM_TILES[name], NORM_BASE[name]
                squares, rstd = norm_tmp(name)
                mean = ("mean", name) in JOB
                for k in range(tiles):
                    if mean and k == tiles - 1:
                        await_freed(act, JOB[("mean", name)])
                    else:
                        act.wait_ge(ln_ready, base + k + 1)
                    if k >= 2:
                        act.wait_ge(ln_used, base - NORM_SKIP[name] + k - 1)
                    act.activation(squares[k % 2], norm_src(name, k), ACT.Square).then_inc(ln_sq, 1)
                n = JOB[("var", name)]
                await_full(act, n)
                if name == "cc":
                    act.wait_ge(saved, 8)
                act.activation(rstd, job_psum(n), ACT.Sqrt, bias=EPSC[:, :]).then_inc(free[n % 2], 1)
                for k in range(tiles):
                    act.wait_ge(ln_mul, base + k + 1)
                    bias = 0.0 if bcol is None else params[:, bcol + k:bcol + k + 1]
                    act.activation(dst[:, k, :], norm_src(name, k), func, bias=bias,
                                   scale=params[:, gcol + k:gcol + k + 1]).then_inc(ln_out, 1)

            act.wait_ge(const_loaded, 64)
            act.wait_ge(set_up, 1)
            norm("ln0", ACT.Identity, 0, KT, X, LN0)
            with act.Fori(0, DEPTH) as layer:
                between_layers(act)
                stage = Stages(act)
                step = Steps(act, scalar_step)

                act.wait_ge(vec_loaded, 16)
                act.activation(EXPA[:, :], VEC[:, V_ALOG:V_ALOG + SSD_HEADS], ACT.Exp)

                def silu_xbc(t):
                    act.wait_ge(conv_done, t + 1)
                    act.wait_ge(saved, t + 1)
                    act.activation(XBC[:, t, 0:SEQ], ACC[:, t % 2, 0:SEQ], ACT.Silu, bias=v(V_SSDB + t))
                    act.activation(by_sample(XBC[:, t, SEQ:TOK]),
                                   samples(ACC[:, t % 2, SSD_S0:SSD_S0 + DEC_BATCH * SSD_SEG], SSD_SEG, 0, DEC_SEQ),
                                   ACT.Silu, bias=v(V_SSDB + t)).then_inc(silu_done, 1)

                for n in range(N_A):
                    name = JOBS[n]
                    if name[0] != "in" or T_GLU <= name[1] < T_Z or name[1] >= T_V:
                        continue
                    j, f = name[1], free[n % 2]
                    await_full(act, n)
                    if T_XBC <= j < T_GATE:
                        t = j - T_XBC
                        if t == 0:
                            act.wait_ge(hist_set, 1)
                        copy(XBC[:, t, SSD_H:SSD_S0], job_psum(n, SEQ))
                        copy(samples(XBC[:, t, SSD_S0:], SSD_SEG, SSD_H, DEC_SEQ),
                             by_sample(job_psum(n, NS, first=SEQ))).then_inc(f, 1)
                    elif j in (T_GATE, T_GATE + 1):
                        act.activation(MIX[:, 6 + j - T_GATE, :], job_psum(n), ACT.Sigmoid).then_inc(f, 1)
                    elif T_Z <= j < T_K:
                        act.activation(MIX[:, j - T_Z, :], job_psum(n), ACT.Silu).then_inc(f, 1)
                    else:
                        dst = (T0 if j == T_KI else QI[:, j - T_QI, :] if j < T_XBC
                               else KTL[:, j - T_K, :] if j < T_Q else QT[:, j - T_Q, :])
                        copy(dst, job_psum(n)).then_inc(f, 1)
                    if j == T_KI:
                        r = slice(DT_ROW, DT_ROW + SSD_HEADS)
                        act.wait_ge(soft_v, 1)
                        act.activation(MIX[r, 5, :], MIX[r, 4, :], ACT.Exp).then_inc(soft_a, 1)
                        act.wait_ge(soft_v, 3)
                        act.activation(MIX[r, 4, :], MIX[r, 4, :], ACT.Ln).then_inc(soft_a, 1)
                    if T_XBC + 1 <= j <= T_GATE:
                        silu_xbc(j - T_XBC - 1)
                for t in range(2):
                    act.wait_ge(conv_done, 6 + t + 1)
                    act.activation(MIX[:, 6 + t, 0:SEQ], ACC[:, t, 0:SEQ], ACT.Identity, bias=v(V_CCB + t))
                    act.activation(by_sample(MIX[:, 6 + t, SEQ:TOK]),
                                   samples(ACC[:, t, CC_S0:CC_LEN - CC_H + CC_H], CC_SEG, 0, DEC_SEQ),
                                   ACT.Identity, bias=v(V_CCB + t)).then_inc(cc_ready, 1)
                norm("cc", ACT.Silu, V_CCG, V_CCBE, MIX[:, 6:8, :])
                stage.end()

                for n, (i, h) in enumerate(SCORED):
                    keys = (i + 1) * P
                    act.wait_ge(idx_full, n + 1)
                    if n >= 2:
                        act.wait_ge(idx_added, n - 1)
                    act.activation(RELU[:, (n % 2) * SEQ:(n % 2) * SEQ + keys], bank(2 * (n % 2), keys), ACT.Relu,
                                   scale=IDX_SCALE).then_inc(idx_relu, 1)
                for g in range(STREAM):
                    act.wait_ge(tr_full, g + 1)
                    if g >= 2:
                        act.wait_ge(tr_used, g - 1)
                    copy(KXT[:, g % 2, 0:256], bank(5 + g % 2, 256)).then_inc(tr_copied, 1)
                act.wait_ge(smp["products"], 1)
                act.wait_ge(idx_added, len(SCORED))
                for half in range(2):
                    act.activation(
                        RELU[:, half * SEQ:(half + 1) * SEQ].rearrange("p (a o t) -> p a o t", o=2, t=P),
                        bank(2 * half, SEQ).rearrange("p (o a t) -> p a o t", o=2, t=P), ACT.Relu, scale=IDX_SCALE)
                act.activation(RELU[:, PAST_LEN:], bank(4, NS), ACT.Relu, scale=IDX_SCALE).then_inc(smp["relu"], 1)
                stage.end()

                for ch, (first, L) in enumerate(CHUNKS):
                    rows = slice(0, L)
                    act.wait_ge(ssd["seg"], ch + 1)
                    act.activation(WS[rows, :], WS[rows, :], ACT.Exp)
                    act.activation(DEC[rows, :, 0:L], DEC[rows, :, 0:L], ACT.Exp)
                    act.activation(E2[:, :, 0:L], bank(5).rearrange("p (j t) -> p j t", t=P)[:, :, 0:L],
                                   ACT.Exp).then_inc(ssd["decay"], 1)
                norm("rms", ACT.Copy, V_RMSG, None, MIX[:, 0:4, :])
                stage.end()

                def exp(n):
                    i, h = BLOCKS[n]
                    keys = (i + 1) * P
                    act.wait_ge(att["masked"], n + 1)
                    act.activation(SC[:, n % 2, 0:keys], SC[:, n % 2, 0:keys], ACT.Exp, bias=NMAX[:, n:n + 1],
                                   accum_out=RSUM[:, n:n + 1]).then_inc(att["exp"], 1)

                def copy_turned(n):
                    i, h = BLOCKS[n]
                    keys = (i + 1) * P
                    act.wait_ge(att["turned"], n + 1)
                    if n >= 2:
                        act.wait_ge(att["out"], n - 1)
                    copy(PROBT[:, n % 2, 0:keys], bank(4, keys)).then_inc(att["copied"], 1)

                for n in range(len(BLOCKS) + 1):
                    if n < len(BLOCKS):
                        exp(n)
                    if n >= 1:
                        copy_turned(n - 1)
                stage.end()

                for g in range(STREAM):
                    act.wait_ge(tr_full, STREAM + g + 1)
                    if g >= 2:
                        act.wait_ge(tr_used, STREAM + g - 1)
                    copy(KTS[:, g % 2, :], bank(5, 1024)).then_inc(tr_copied, 1)
                act.wait_ge(smp["max"], 1)
                act.activation(PR, bank(0, SKEYS), ACT.Exp, bias=SMAX, accum_out=SSUM).then_inc(smp["exp"], 1)
                act.wait_ge(smp["turned"], 1)
                copy(PRT[:, 0:PAGES, :], bank(0, PAGES * P)).then_inc(smp["copied"], 1)
                copy(PRT[0:NS, PAGES, :], bank(4, P, slice(0, NS))).then_inc(smp["copied"], 1)
                stage.end()

                norm("ln1", ACT.Identity, V_LN1G, V_LN1B, X)
                stage.end()

                def silu_gate(j):
                    n = g * 2 * FG + 2 * j
                    act.wait_ge(u_conv, n + 1)
                    if g * FG + j >= 1:
                        act.wait_ge(hid_done, g * FG + j)
                    act.activation(GATE[:, 0:FFN_LEN - FFN_H], FACC[:, 0, 0:FFN_LEN - FFN_H], ACT.Silu,
                                   bias=v(V_FFB + n)).then_inc(gate_done, 1)

                for g in range(GROUPS):
                    for j in range(2 * FG):
                        n, m = JOB[("up", g, j)], g * 2 * FG + j
                        await_full(act, n)
                        act.wait_ge(u_hist, m + 1)
                        copy(U[:, m % 2, FFN_H:FFN_S0], job_psum(n, SEQ))
                        copy(samples(U[:, m % 2, FFN_S0:], FFN_SEG, FFN_H, DEC_SEQ),
                             by_sample(job_psum(n, NS, first=SEQ))).then_inc(free[n % 2], 1)
                        if j % 2:
                            silu_gate(j // 2)
                norm("ln2", ACT.Identity, V_LN2G, V_LN2B, X)
                stage.end()

        @block.vector
        def _(dve):
            def norm(name):
                tiles, base = NORM_TILES[name], NORM_BASE[name]
                rstd = norm_tmp(name)[1]
                if ("mean", name) in JOB:
                    n = JOB[("mean", name)]
                    await_full(dve, n)
                    for k in range(tiles):
                        s = norm_src(name, k)
                        dve.tensor_tensor(s, s, job_psum(n), ALU.subtract).then_inc(
                            free[n % 2] if k == tiles - 1 else ln_ready, 1)
                await_freed(dve, JOB[("var", name)])
                if ("mean", name) in JOB:
                    dve.drain().then_inc(ln_ready, 1)
                dve.reciprocal(rstd, rstd).then_inc(ln_std, 1)
                dve.wait_ge(ln_std, NORM_ORDER[name])
                for k in range(tiles):
                    s = norm_src(name, k)
                    dve.tensor_tensor(s, s, rstd, ALU.mult).then_inc(ln_mul, 1)

            dve.wait_ge(const_loaded, 64)
            norm("ln0")
            with dve.Fori(0, DEPTH) as layer:
                between_layers(dve)
                stage = Stages(dve)
                step = Steps(dve, vector_step)
                dve.wait_ge(vec_loaded, 16)

                def convolve(acc, src, taps, col, done):
                    w = acc.shape[-1]
                    step.then_wait(dve.tensor_scalar(acc, src[:, 0:w], v(col), None, ALU.mult))
                    for k in range(1, taps):
                        ins = dve.scalar_tensor_tensor(out=acc, in0=src[:, k:k + w], scalar=v(col + k), in1=acc,
                                                       op0=ALU.mult, op1=ALU.add)
                        if k < taps - 1:
                            step.then_wait(ins)
                    ins.then_inc(done, 1)

                def rotate(raw, n):
                    await_full(dve, n)
                    step.then_wait(dve.tensor_tensor(raw, raw, c("cos"), ALU.mult))
                    step.then_wait(dve.tensor_tensor(ROPE, job_psum(n), c("sin"), ALU.mult))
                    dve.tensor_tensor(raw, raw, ROPE, ALU.add).then_inc(free[n % 2], 1)

                for n in range(N_A):
                    name = JOBS[n]
                    if name == ("in", T_KI):
                        r = slice(DT_ROW, DT_ROW + SSD_HEADS)
                        await_freed(dve, n)
                        step.then_wait(dve.tensor_scalar(T0[r, :], T0[r, :], v(V_DTB, r), None, ALU.add))
                        dve.scalar_tensor_tensor(out=MIX[r, 4, :], in0=T0[r, :], scalar=-1.0, in1=T0[r, :],
                                                 op0=ALU.mult, op1=ALU.min).then_inc(soft_v, 1)
                        dve.wait_ge(soft_a, 1)
                        dve.tensor_scalar(MIX[r, 4, :], MIX[r, 5, :], 1.0, None, ALU.add).then_inc(soft_v, 1)
                        dve.wait_ge(soft_v, 2)
                        dve.scalar_tensor_tensor(out=MIX[r, 5, :], in0=MIX[r, 4, :], scalar=-1.0, in1=MIX[r, 5, :],
                                                 op0=ALU.add, op1=ALU.subtract).then_inc(soft_v, 1)
                        dve.wait_ge(soft_a, 2)
                        dve.wait_ge(soft_v, 3)
                        step.then_wait(dve.scalar_tensor_tensor(out=T0[r, :], in0=T0[r, :], scalar=0.0,
                                                                in1=MIX[r, 4, :], op0=ALU.max, op1=ALU.add))
                        dve.tensor_tensor(T0[r, :], T0[r, :], MIX[r, 5, :], ALU.subtract).then_inc(soft_v, 1)
                    elif name[0] == "dup":
                        await_full(dve, n)
                        dve.tensor_tensor(KID, job_psum(n), c("cos"), ALU.mult).then_inc(free[n % 2], 1)
                    elif name[0] == "rotdup":
                        await_full(dve, n)
                        dve.tensor_tensor(ROPE, job_psum(n), c("sin"), ALU.mult).then_inc(free[n % 2], 1)
                        await_freed(dve, n)
                        await_freed(dve, n - 1)
                        step.then_wait(dve.tensor_tensor(KID, KID, ROPE, ALU.add))
                    elif name[0] == "turn":
                        await_full(dve, n)
                        for rows, ch, a, w in ((P, slice(0, NCHUNK), 0, NCHUNK * P),
                                               (NS, slice(NCHUNK, NCHUNK + 1), NCHUNK * P, P)):
                            t = job_psum(n, w, slice(0, rows), first=a).rearrange("p (c m) -> p c m", m=P)
                            dve.tensor_copy(DTT[0:rows, ch, :], t[:, :, DT_ROW:DT_ROW + SSD_HEADS])
                            ins = dve.tensor_scalar(WIT[0:rows, ch, :], t[:, :, WI_ROW:WI_ROW + IDX_HEADS],
                                                    IDX_HEADS ** -0.5, None, ALU.mult)
                        ins.then_inc(free[n % 2], 1)
                    elif name[0] == "rot":
                        r = name[1]
                        await_freed(dve, JOB[("in", r)])
                        rotate(QI[:, r - T_QI, :] if r < T_XBC else KTL[:, r - T_K, :] if r < T_Q
                               else QT[:, r - T_Q, :], n)
                    elif T_XBC <= name[1] < T_GATE:
                        t = name[1] - T_XBC
                        await_freed(dve, n)
                        if t >= 2:
                            dve.wait_ge(silu_done, t - 1)
                        convolve(ACC[:, t % 2, 0:SSD_LEN - SSD_H], XBC[:, t, :], SSD_W, V_SSDW + t * SSD_W, conv_done)
                    elif T_GLU <= name[1] < T_Z:
                        t = name[1] - T_GLU
                        await_full(dve, n)
                        if t == 0:
                            dve.wait_ge(hist_set, 1)
                        await_freed(dve, JOB[("in", T_GATE + t)])
                        dve.tensor_tensor(CC[:, t, CC_H:CC_S0], job_psum(n, SEQ), MIX[:, 6 + t, 0:SEQ], ALU.mult)
                        dve.tensor_tensor(samples(CC[:, t, CC_S0:], CC_SEG, CC_H, DEC_SEQ),
                                          by_sample(job_psum(n, NS, first=SEQ)), by_sample(MIX[:, 6 + t, SEQ:TOK]),
                                          ALU.mult).then_inc(free[n % 2], 1)
                        if t == 1:
                            for t in range(2):
                                dve.wait_ge(silu_done, 5 + t)
                                await_freed(dve, JOB[("in", T_GLU + t)])
                                convolve(ACC[:, t, 0:CC_LEN - CC_H], CC[:, t, :], CC_W, V_CCW + t * CC_W, conv_done)
                    elif name[1] >= T_V:
                        t = name[1] - T_V
                        await_full(dve, n)
                        dve.tensor_copy(VTOK[:, 0:NCHUNK, t * P:(t + 1) * P],
                                        job_psum(n, SEQ).rearrange("p (c m) -> p c m", m=P))
                        dve.tensor_copy(VTOK[0:NS, NCHUNK, t * P:(t + 1) * P],
                                        job_psum(n, P, slice(0, NS), first=SEQ)).then_inc(free[n % 2], 1)
                norm("cc")
                stage.end()

                for n, (i, h) in enumerate(SCORED):
                    keys = (i + 1) * P
                    sel = SEL[:, SEL_AT[i]:SEL_AT[i] + keys]
                    relu = RELU[:, (n % 2) * SEQ:(n % 2) * SEQ + keys]
                    dve.wait_ge(idx_relu, n + 1)
                    w = WIT[:, i, h:h + 1]
                    if h == 0:
                        ins = dve.tensor_scalar(sel, relu, w, None, ALU.mult)
                    else:
                        dve.wait_ge(idx_added, n)
                        ins = dve.scalar_tensor_tensor(out=sel, in0=relu, scalar=w, in1=sel, op0=ALU.mult, op1=ALU.add)
                    ins.then_inc(idx_added, 1)
                    if h == IDX_HEADS - 1:
                        dve.wait_ge(idx_added, n + 1)
                        d = sel[:, keys - P:keys]
                        step.then_wait(dve.tensor_tensor(d, d, c("causal"), ALU.add))
                dve.wait_ge(pool_step, 1)
                dve.wait_ge(smp["swap"], 2)
                qis = QIS.rearrange("p (b x) -> p b x", x=P + 16)
                for h in range(IDX_HEADS):
                    for half in range(2):
                        r = slice(half * HEAD, half * HEAD + HEAD)
                        src = (QI[r, h // 2, SEQ:TOK] if half == h % 2
                               else bank(7, 512, r)[:, 64 * (h // 2):64 * (h // 2) + NS])
                        ins = dve.tensor_copy(qis[r, :, h * DEC_SEQ:(h + 1) * DEC_SEQ], by_sample(src))
                ins.then_inc(smp["q"], 1)
                step.then_wait(dve.tensor_tensor(WCOL[:, 0:IDX_HEADS], bank(7)[:, 256:256 + IDX_HEADS], c("hsel"),
                                                 ALU.mult))
                step.then_wait(dve.reduce_sum(WCOL[:, 4:5], WCOL[:, 0:IDX_HEADS], AX.X))
                dve.tensor_scalar(WMAT, c("repT"), WCOL[:, 4:5], None, ALU.mult).then_inc(smp["wmat"], 1)
                dve.wait_ge(smp["scores"], 1)
                rows = slice(0, NS)
                dve.tensor_copy(SELS[rows, 0:PAST_LEN], bank(0, PAST_LEN, rows))
                dve.tensor_tensor(SELS[rows, PAST_LEN:], bank(4, NS, rows), c("newmask", NS), ALU.add)
                stage.end()

                def choose():
                    jobs = [(SELS[0:NS, :], NS)]
                    jobs += [(SEL[:, SEL_AT[i]:SEL_AT[i] + (i + 1) * P], P) for i in range(2, NCHUNK)]
                    for sel, rows in jobs:
                        for _ in range(TOPK // 8):
                            step.then_wait(dve.max(T8[0:rows, :], sel))
                            step.then_wait(dve.match_replace(sel, T8[0:rows, :], sel, TAKEN))
                            yield
                        step.then_wait(dve.tensor_scalar(sel, sel, TAKEN / 2, BIG, ALU.is_gt, ALU.mult))
                        yield

                choice = choose()

                def choose_some(n):
                    for _ in range(n):
                        next(choice, None)

                for ch, (first, L) in enumerate(CHUNKS):
                    cols, rows, last = slice(first, first + L), slice(0, L), ch == NCHUNK
                    step.then_wait(dve.scalar_tensor_tensor(out=DA[rows, :], in0=DTT[rows, ch, :], scalar=-1.0,
                                                            in1=EXPA[rows, :], op0=ALU.mult, op1=ALU.mult))
                    dve.wait_ge(ssd["turned"], ch + 1)
                    dve.tensor_copy(BTOK[rows, :], bank(1, P, rows))
                    dve.tensor_tensor(XDT[rows, :, :], bank(0, 512, rows).rearrange("p (h d) -> p h d", d=HEAD),
                                      DTT[rows, ch, :].unsqueeze(2).broadcast_to([L, SSD_HEADS, HEAD]), ALU.mult
                                      ).then_inc(ssd["taken"], 1)
                    choose_some(8)
                    dve.wait_ge(ssd["sums"], ch + 1)
                    step.then_wait(dve.tensor_copy(CUM[rows, :], bank(2, 8, rows)))
                    dve.tensor_tensor(WS[rows, :], bank(2, 512, rows)[:, 8:16], CUM[rows, :], ALU.subtract)
                    mask = c("causalT_s", L)[:, 0:L] if last else c("causalT")
                    for h in range(SSD_HEADS):
                        ins = dve.scalar_tensor_tensor(
                            out=DEC[rows, h, 0:L], in0=bank(3 + h // 4, 512, rows)[:, (h % 4) * P:(h % 4) * P + L],
                            scalar=CUM[rows, h:h + 1], in1=mask, op0=ALU.subtract, op1=ALU.add)
                    ins.then_inc(ssd["seg"], 1)
                    choose_some(8)
                    dve.wait_ge(ssd["decay"], ch + 1)
                    for g in range(2):
                        d = DEC[rows, 4 * g:4 * g + 4, 0:L]
                        cb = bank(2 + 5 * g, 512, rows)[:, 256:256 + L]
                        dve.tensor_tensor(d, d, cb.unsqueeze(1).broadcast_to([L, 4, L]), ALU.mult)
                    dve.tensor_tensor(CE[:, :, 0:L], XBC[:, 5, cols].unsqueeze(1).broadcast_to([P, 4, L]),
                                      E2[:, :, 0:L], ALU.mult)
                    ins = dve.tensor_tensor(XW[rows, :, :], XDT[rows, :, :],
                                            WS[rows, :].unsqueeze(2).broadcast_to([L, SSD_HEADS, HEAD]), ALU.mult)
                    ins.then_inc(ssd["weighed"], 1)
                    choose_some(8)
                    dve.wait_ge(ssd["y"], ch + 1)
                    for t in range(4):
                        ins = dve.scalar_tensor_tensor(out=YT[:, t, 0:L], in0=XBC[:, t, cols], scalar=v(V_D + t),
                                                       in1=bank(6 - t // 2)[:, (t % 2) * P:(t % 2) * P + L], op0=ALU.mult, op1=ALU.add)
                    step.then_wait(ins)
                    y = MIX[:, 0:4, cols]
                    dve.tensor_tensor(y, y, YT[:, :, 0:L], ALU.mult)
                    if not last:
                        dve.wait_ge(ssd["h"], ch + 1)
                        if ch == 0:
                            dve.wait_ge(pool_step, 2)
                        step.then_wait(dve.tensor_tensor(HP[:, :, :], HP[:, :, :],
                                                         E2[:, :, L - 1:L].broadcast_to([P, 4, HEAD]), ALU.mult))
                        dve.tensor_tensor(HP[:, :, :], HP[:, :, :],
                                          bank(7, 256).rearrange("p (j d) -> p j d", d=HEAD), ALU.add
                                          ).then_inc(ssd["state"], 1)
                        dve.wait_ge(ssd["state"], ch + 1)
                    else:
                        for b in range(DEC_BATCH):
                            if b >= 2:
                                dve.wait_ge(ssd["h"], NCHUNK + b - 1)
                            dve.tensor_scalar(XWB[rows, b % 2, :], XW[rows, :, :].rearrange("p h d -> p (h d)"),
                                              c("bsel", NS)[:, b:b + 1], None, ALU.mult).then_inc(ssd["masked"], 1)
                        dve.wait_ge(ssd["h"], NCHUNK + DEC_BATCH)
                        for j in range(4):
                            e = E2[:, j, 0:NS].rearrange("p (b t) -> p b t", t=DEC_SEQ)[:, :, DEC_SEQ - 1:DEC_SEQ]
                            ins = dve.tensor_tensor(HS[:, :, j, :], HS[:, :, j, :],
                                                    e.broadcast_to([P, DEC_BATCH, HEAD]), ALU.mult)
                        step.then_wait(ins)
                        dve.tensor_tensor(HS[:, :, :, :].rearrange("p b j d -> p (b j d)"),
                                          HS[:, :, :, :].rearrange("p b j d -> p (b j d)"), bank(2, 2048), ALU.add
                                          ).then_inc(ssd["state"], 1)
                dve.drain().then_inc(ln_ready, 4)
                norm("rms")
                dve.wait_ge(ln_mul, NORM_BASE["rms"] + NORM_TILES["rms"])
                for _ in choice:
                    pass
                stage.end()

                def mask(n):
                    i, h = BLOCKS[n]
                    keys = (i + 1) * P
                    s, ps = SC[:, n % 2, 0:keys], bank(2 * (n % 2), keys)
                    dve.wait_ge(att["scores"], n + 1)
                    if n >= 2:
                        dve.wait_ge(att["turned"], n - 1)
                    if i >= 2:
                        step.then_wait(dve.scalar_tensor_tensor(
                            out=s, in0=ps, scalar=ATT_SCALE, in1=SEL[:, SEL_AT[i]:SEL_AT[i] + keys],
                            op0=ALU.mult, op1=ALU.add))
                    else:
                        if i:
                            dve.tensor_scalar(s[:, 0:keys - P], ps[:, 0:keys - P], ATT_SCALE, None, ALU.mult)
                        step.then_wait(dve.scalar_tensor_tensor(
                            out=s[:, keys - P:], in0=ps[:, keys - P:], scalar=ATT_SCALE, in1=c("causal"),
                            op0=ALU.mult, op1=ALU.add))
                    dve.tensor_reduce(NMAX[:, n:n + 1], s, AX.X, ALU.max, negate=True).then_inc(att["masked"], 1)

                def normalise(n):
                    i, h = BLOCKS[n]
                    s = SC[:, n % 2, 0:(i + 1) * P]
                    dve.wait_ge(att["exp"], n + 1)
                    step.then_wait(dve.reciprocal(RSUM[:, n:n + 1], RSUM[:, n:n + 1]))
                    dve.tensor_scalar(s, s, RSUM[:, n:n + 1], None, ALU.mult).then_inc(att["normed"], 1)

                def take_out(i):
                    dve.wait_ge(att["out"], 4 * (i + 1))
                    for t in range(2):
                        ins = dve.tensor_copy(MIX[:, 4 + t, i * P:(i + 1) * P], bank(6 + t, P))
                    ins.then_inc(att["out_read"], 1)

                for n in range(len(BLOCKS) + 1):
                    if n < len(BLOCKS):
                        mask(n)
                    if n >= 1:
                        normalise(n - 1)
                    if n >= 4 and n % 4 == 2:
                        take_out(n // 4 - 1)
                take_out(NCHUNK - 1)
                stage.end()

                dve.wait_ge(pool_step, 3)
                kq = KQ.rearrange("p (b x) -> p b x", x=2 * P + 16)
                for h in range(ATT_HEADS):
                    r, t = slice((h % 2) * HEAD, (h % 2) * HEAD + HEAD), h // 2
                    ins = dve.tensor_scalar(kq[r, :, t * P + h * DEC_SEQ:t * P + (h + 1) * DEC_SEQ],
                                            by_sample(QT[r, t, SEQ:TOK]), ATT_SCALE, None, ALU.mult)
                ins.then_inc(smp["kq"], 1)
                dve.wait_ge(smp["logits"], 1)
                dve.tensor_reduce(SMAX, bank(0, SKEYS), AX.X, ALU.max, negate=True).then_inc(smp["max"], 1)
                dve.wait_ge(smp["exp"], 1)
                step.then_wait(dve.reciprocal(SSUM, SSUM))
                dve.tensor_scalar(PR, PR, SSUM, None, ALU.mult).then_inc(smp["normed"], 1)
                dve.wait_ge(v_used, STREAM)
                for h in range(ATT_HEADS):
                    r, t = slice((h % 2) * HEAD, (h % 2) * HEAD + HEAD), h // 2
                    src = bank(7, 512, r)[:, t * P:(t + 1) * P].rearrange("p (b x) -> p b x", x=16)
                    dve.tensor_copy(by_sample(MIX[r, 4 + t, SEQ:TOK]), src[:, :, h * DEC_SEQ:(h + 1) * DEC_SEQ])
                stage.end()

                for j in range(KT):
                    n = JOB[("out", j)]
                    await_full(dve, n)
                    dve.scalar_tensor_tensor(out=X[:, j, :], in0=X[:, j, :], scalar=ALPHA, in1=job_psum(n),
                                             op0=ALU.mult, op1=ALU.add).then_inc(free[n % 2], 1)
                await_freed(dve, JOB[("out", KT - 1)])
                await_freed(dve, JOB[("out", KT - 2)])
                norm("ln1")
                stage.end()

                wide = FFN_LEN - FFN_H
                for g in range(GROUPS):
                    for j in range(2 * FG):
                        n, m = JOB[("up", g, j)], g * 2 * FG + j
                        await_freed(dve, n)
                        if j % 2 == 0 and m:
                            dve.wait_ge(gate_done, m // 2)
                        convolve(FACC[:, j % 2, 0:wide], U[:, m % 2, :], FFN_W, V_FFW + m * FFN_W, u_conv)
                        if j % 2 == 0:
                            continue
                        dve.wait_ge(gate_done, m // 2 + 1)
                        dve.wait_ge(u_conv, m + 1)
                        if g and j == 1:
                            await_full(dve, JOB[("down", g - 1, KT - 1)])
                        acc, h = FACC[:, 1, :], HID[:, j // 2, :]
                        dve.scalar_tensor_tensor(out=h[:, 0:SEQ], in0=acc[:, 0:SEQ], scalar=v(V_FFB + m),
                                                 in1=GATE[:, 0:SEQ], op0=ALU.add, op1=ALU.mult)
                        s = slice(FFN_S0, FFN_S0 + DEC_BATCH * FFN_SEG)
                        dve.scalar_tensor_tensor(out=by_sample(h[:, SEQ:TOK]), in0=samples(acc[:, s], FFN_SEG, 0, DEC_SEQ),
                                                 scalar=v(V_FFB + m), in1=samples(GATE[:, s], FFN_SEG, 0, DEC_SEQ),
                                                 op0=ALU.add, op1=ALU.mult).then_inc(hid_done, 1)
                    for j in range(KT):
                        n = JOB[("down", g, j)]
                        await_full(dve, n)
                        if g == 0:
                            ins = dve.scalar_tensor_tensor(out=MIX[:, j, :], in0=X[:, j, :], scalar=ALPHA,
                                                           in1=job_psum(n), op0=ALU.mult, op1=ALU.add)
                        else:
                            ins = dve.tensor_tensor(MIX[:, j, :], MIX[:, j, :], job_psum(n), ALU.add)
                        ins.then_inc(free[n % 2], 1)
                await_freed(dve, JOB[("down", GROUPS - 1, KT - 1)])
                await_freed(dve, JOB[("down", GROUPS - 1, KT - 2)])
                norm("ln2")
                stage.end()


def _constants():
    a = np.zeros((P, NCONST), np.float32)

    def put(name, x):
        at, w = CONSTS[name]
        assert x.shape[1] == w
        a[:x.shape[0], at:at + w] = x

    t = np.arange(P)
    put("ident", np.eye(P))
    put("causal", np.where(t[None, :] > t[:, None], BIG, 0.0))
    put("causalT", np.where(t[:, None] > t[None, :], BIG, 0.0))
    put("tri", (t[:, None] <= t[None, :]) * 1.0)
    rot = np.zeros((P, P))
    for o in range(P):
        if o % HEAD < HEAD // 2:
            rot[o + HEAD // 2, o] = -1.0
        else:
            rot[o - HEAD // 2, o] = 1.0
    put("rot", rot)
    dup = (t[:, None] == t[None, :] % HEAD) * 1.0
    put("dup", dup)
    put("rotdup", rot @ np.eye(P)[:, t % HEAD])
    put("swap", np.eye(P)[:, (t + HEAD) % P])
    s = np.arange(NS)
    same = s[:, None] // DEC_SEQ == s[None, :] // DEC_SEQ
    put("causalT_s", np.where(same & (s[:, None] <= s[None, :]), 0.0, BIG))
    put("tri_s", (same & (s[:, None] <= s[None, :])) * 1.0)
    put("block_s", same * 1.0)
    put("newmask", np.where(same & (s[None, :] <= s[:, None]), 0.0, BIG))
    row = np.arange(ROWS)
    owner = row // 16 * DEC_SEQ + row % DEC_SEQ
    put("rep", (s[:, None] == owner[None, :]) * 1.0)
    put("repT", (owner[:, None] == s[None, :]) * 1.0)
    put("hsel", (row[:, None] // DEC_SEQ % ATT_HEADS == np.arange(IDX_HEADS)[None, :]) * 1.0)
    put("bsel", (s[:, None] // DEC_SEQ == np.arange(DEC_BATCH)[None, :]) * 1.0)
    pos = np.concatenate([np.arange(SEQ), PAST_LEN + np.arange(NS) % DEC_SEQ]).astype(np.float32)
    half = HEAD // 2
    inv = np.power(10000.0, (-np.arange(half, dtype=np.float32) / np.float32(half)).astype(np.float64)).astype(np.float32)
    ang = (pos[None, :] * inv[t % half][:, None]).astype(np.float64)
    put("cos", np.cos(ang))
    put("sin", np.sin(ang))
    return a


def _tiles(w, m_tiles):
    d, k, m = w.shape
    return np.ascontiguousarray(w.reshape(d, k // P, P, m_tiles, P).transpose(0, 3, 2, 1, 4)).reshape(
        d, m_tiles, P, (k // P) * P)


def _channels(x):
    return np.moveaxis(x.reshape(*x.shape[:-1], x.shape[-1] // P, P), -1, 0)


def kernel(**inputs):
    import concourse.bacc as bacc
    from concourse.bass_utils import run_bass_kernel_spmd

    a = {k: np.asarray(v) for k, v in inputs.items()}
    sizes = np.cumsum([0, SSD_INNER, SSD_CONV, SSD_HEADS, 256, 256, 256, 256, HEAD, IDX_HEADS, 2 * CC_WIDTH])
    z, xbc, dt, q, k, v, qi, ki, wi, glu = (a["w_in"][:, :, s:e] for s, e in zip(sizes, sizes[1:]))
    first = np.zeros((DEPTH, D_MODEL, P), np.float32)
    first[:, :, 0:HEAD], first[:, :, DT_ROW:DT_ROW + SSD_HEADS], first[:, :, WI_ROW:WI_ROW + IDX_HEADS] = ki, dt, wi
    w_in = _tiles(np.concatenate([first, qi, xbc, glu[:, :, CC_WIDTH:], glu[:, :, :CC_WIDTH], z, k, q, v], 2), N_IN)
    order = np.stack([np.arange(FF) + FF, np.arange(FF)], 1).reshape(-1)
    up = a["ffn_w_up"].reshape(DEPTH, D_MODEL, 2 * FF, P)[:, :, order].reshape(DEPTH, D_MODEL, 2 * D_FF)
    down = a["ffn_w_down"].reshape(DEPTH, GROUPS, FG * P, D_MODEL)
    w_down = np.stack([_tiles(down[:, g], KT) for g in range(GROUPS)], 1).reshape(DEPTH, GROUPS * KT, P, FG * P)
    vec = np.zeros((DEPTH, P, NVEC), np.float32)
    for l in range(DEPTH):
        def put(col, x):
            x = x.reshape(x.shape[0], -1)
            vec[l, :x.shape[0], col:col + x.shape[1]] = x

        def per_tile(name, perm=None):
            x = _channels(a[name][l])
            x = x if perm is None else x[..., perm]
            return x if x.ndim == 2 else x.transpose(0, 2, 1)

        put(V_SSDW, per_tile("ssd_conv_w")), put(V_SSDB, per_tile("ssd_conv_b"))
        put(V_CCW, per_tile("cc_conv_w")), put(V_CCB, per_tile("cc_conv_b"))
        put(V_CCG, per_tile("cc_ln_g")), put(V_CCBE, per_tile("cc_ln_b"))
        put(V_RMSG, per_tile("ssd_norm_g"))
        put(V_D, _channels(np.repeat(a["ssd_d"][l], HEAD)))
        put(V_LN1G, per_tile("ln1_g")), put(V_LN1B, per_tile("ln1_b"))
        put(V_LN2G, per_tile("ln2_g")), put(V_LN2B, per_tile("ln2_b"))
        put(V_FFW, per_tile("ffn_conv_w", order)), put(V_FFB, per_tile("ffn_conv_b", order))
        put(V_ALOG, np.broadcast_to(a["ssd_a_log"][l], (P, SSD_HEADS)))
        vec[l, DT_ROW:DT_ROW + SSD_HEADS, V_DTB] = a["ssd_dt_bias"][l]
    x = np.concatenate([a["x_prompt"].reshape(SEQ, D_MODEL), a["x_sample"].reshape(NS, D_MODEL)])

    def state(name, perm=None):
        s = _channels(a[name])
        s = s if perm is None else s[..., perm]
        return np.ascontiguousarray(s.transpose(2, 0, 4, 1, 3)).reshape(DEPTH, P, s.shape[-1], -1)

    ssm = np.ascontiguousarray(a["state_ssm"].reshape(DEC_BATCH, DEPTH, 2, 4, HEAD, SSD_STATE)
                               .transpose(1, 2, 5, 0, 3, 4)).reshape(DEPTH, P, DEC_BATCH, 4, HEAD)
    n_pool = a["cache_k"].shape[0]
    arrays = {
        "xT": np.ascontiguousarray(_channels(x).transpose(0, 2, 1)),
        "w_in": w_in, "w_out": _tiles(a["w_out"], KT), "w_up": _tiles(up, 2 * FF), "w_down": w_down, "vec": vec,
        "ln0": np.concatenate([_channels(a["ln0_g"]), _channels(a["ln0_b"])], 1), "const": _constants(),
        "pages": np.ascontiguousarray(a["page_table"].reshape(1, -1)),
        "cache_k": a["cache_k"].reshape(n_pool, DEPTH, PAGE, 256), "cache_v": a["cache_v"].reshape(n_pool, DEPTH, PAGE, 256),
        "cache_kidx": a["cache_kidx"], "ssm_in": ssm, "ssd_in": state("state_ssd_conv"),
        "cc_in": state("state_cc_conv"), "ffn_in": state("state_ffn_conv", order),
    }
    outs = {
        "yT": (P, KT, TOK), "kT_out": (DEPTH, 2, P, TOK), "v_out": (DEPTH, P, NCHUNK + 1, 256),
        "ki_out": (DEPTH, HEAD, TOK), "ssm_p": (DEPTH, P, 4, HEAD), "ssm_s": (DEPTH, P, DEC_BATCH, 4, HEAD),
        "ssd_out": (DEPTH, P, 6, SSD_H * (1 + DEC_BATCH)), "cc_out": (DEPTH, P, 2, CC_H * (1 + DEC_BATCH)),
        "ffn_out": (DEPTH, P, 2 * FF, FFN_H * (1 + DEC_BATCH)),
    }
    nc = bacc.Bacc("TRN2", target_bir_lowering=False, num_devices=1)
    args = [nc.dram_tensor(n, x.shape, mybir.dt.from_np(x.dtype), kind="ExternalInput").ap() for n, x in arrays.items()]
    args += [nc.dram_tensor(n, s, F32, kind="ExternalOutput").ap() for n, s in outs.items()]
    build(nc, *args)
    r = run_bass_kernel_spmd(nc, [arrays], core_ids=[0]).results[0]

    y = r["yT"].transpose(2, 1, 0).reshape(TOK, D_MODEL)
    kk = r["kT_out"].reshape(DEPTH, ATT_HEADS, HEAD, TOK).transpose(0, 3, 1, 2)
    vv = np.concatenate([r["v_out"][:, :, :NCHUNK].transpose(0, 2, 1, 3).reshape(DEPTH, SEQ, 256),
                         r["v_out"][:, :NS, NCHUNK]], 1).reshape(DEPTH, TOK, ATT_HEADS, HEAD)
    ki_ = r["ki_out"].transpose(0, 2, 1)

    def by_group(x):
        s = x[:, SEQ:].reshape(DEPTH, DEC_BATCH, DEC_SEQ, *x.shape[2:])
        return x[None, :, :SEQ], np.moveaxis(s, 1, 0)

    def ssm_of(x, n):
        return x.reshape(DEPTH, 2, SSD_STATE, n, 4, HEAD).transpose(3, 0, 1, 4, 5, 2).reshape(
            n, DEPTH, SSD_HEADS, HEAD, SSD_STATE)

    def conv_of(x, h, perm=None):
        x = x.reshape(DEPTH, P, x.shape[2], 1 + DEC_BATCH, h)
        if perm is not None:
            x = x[:, :, np.argsort(perm)]
        x = x.transpose(3, 0, 4, 2, 1).reshape(1 + DEC_BATCH, DEPTH, h, -1)
        return x[:1], x[1:]

    (p_k, s_k), (p_v, s_v), (p_ki, s_ki) = by_group(kk), by_group(vv), by_group(ki_)
    p_ssd, s_ssd = conv_of(r["ssd_out"], SSD_H)
    p_cc, s_cc = conv_of(r["cc_out"], CC_H)
    p_ff, s_ff = conv_of(r["ffn_out"], FFN_H, order)
    res = (y[None, :SEQ], y[SEQ:].reshape(DEC_BATCH, DEC_SEQ, D_MODEL), p_k, p_v, p_ki,
           ssm_of(r["ssm_p"][:, :, None], 1), p_ssd, p_cc, p_ff, s_k, s_v, s_ki, ssm_of(r["ssm_s"], DEC_BATCH),
           s_ssd, s_cc, s_ff)
    return tuple(np.ascontiguousarray(x) for x in res)
```
